# Optimizing a Trainium2 kernel written in Bass

```python
import jax, jax.numpy as jnp
from jax import lax
import numpy as np

D_MODEL = 1024
BATCH = 1
SEQ = 512
DEPTH = 1
DEC_BATCH = 8
DEC_SEQ = 8
PAST_LEN = 4096
PAGE_SIZE = 128

HEAD_DIM = 64
N_HEADS_FOX = 8
N_HEADS_DIL = 8
DIL_PATTERNS = ((128, 1), (512, 4), (2048, 16))
N_GROUPS = len(DIL_PATTERNS)
D_FOX = N_HEADS_FOX * HEAD_DIM
D_DIL = N_HEADS_DIL * HEAD_DIM
D_FF = 4 * D_MODEL
ROPE_THETA = 10000.0
EPS = 1e-6
Q_BLOCK = 128
FORGET_BIAS_MIN = 2.0
FORGET_BIAS_MAX = 9.0
D_IN = 3 * D_FOX + N_HEADS_FOX + N_GROUPS * 3 * D_DIL + 2 * D_MODEL

kernel_name = "fox_dilated_gated_hybrid_step"

def rmsnorm(x, g):
    xf = x.astype(jnp.float32)
    y = xf * lax.rsqrt(jnp.mean(xf * xf, axis=-1, keepdims=True) + EPS)
    return (y * g.astype(jnp.float32)).astype(x.dtype)

def rope(x, pos):
    half = HEAD_DIM // 2
    inv = ROPE_THETA ** (-jnp.arange(half, dtype=jnp.float32) / half)
    ang = pos.astype(jnp.float32)[:, None] * inv[None, :]
    cos = jnp.cos(ang)[None, :, None, :]
    sin = jnp.sin(ang)[None, :, None, :]
    xf = x.astype(jnp.float32)
    x1, x2 = xf[..., :half], xf[..., half:]
    return jnp.concatenate([x1 * cos - x2 * sin, x2 * cos + x1 * sin], axis=-1).astype(x.dtype)

def softmax_stats(s, valid):
    s = jnp.where(valid, s, -jnp.inf)
    m = jnp.max(s, axis=-1, keepdims=True)
    p = jnp.exp(s - m)
    den = jnp.sum(p, axis=-1, keepdims=True)
    return p / den, (m + jnp.log(den))[..., 0]

def project(x, pos, lp):
    (norm1_g, w_in, b_forget, qn_fox_g, kn_fox_g, qn_dil_g, kn_dil_g,
     _wa, _wb, _wo, _n2, _wu, _wd) = lp
    B, S, _ = x.shape
    xn = rmsnorm(x, norm1_g)
    proj = xn @ w_in
    bounds = np.cumsum([D_FOX] * 3 + [N_HEADS_FOX] + [D_DIL] * (3 * N_GROUPS) + [D_MODEL])
    parts = jnp.split(proj, bounds, axis=-1)
    heads = lambda t, h: t.reshape(B, S, h, HEAD_DIM)
    q_f = rmsnorm(heads(parts[0], N_HEADS_FOX), qn_fox_g)
    k_f = rmsnorm(heads(parts[1], N_HEADS_FOX), kn_fox_g)
    v_f = heads(parts[2], N_HEADS_FOX)
    logf = jax.nn.log_sigmoid((parts[3] + b_forget).astype(jnp.float32))
    dil = []
    for g in range(N_GROUPS):
        q = rope(rmsnorm(heads(parts[4 + 3 * g], N_HEADS_DIL), qn_dil_g[g]), pos)
        k = rope(rmsnorm(heads(parts[5 + 3 * g], N_HEADS_DIL), kn_dil_g[g]), pos)
        v = heads(parts[6 + 3 * g], N_HEADS_DIL)
        dil.append((q, k, v))
    return q_f, k_f, v_f, logf, dil, parts[4 + 3 * N_GROUPS], parts[5 + 3 * N_GROUPS]

def finish(x, o_fox, o_dil, gate_a, gate_b, lp):
    (_n1, _wi, _bf, _qf, _kf, _qd, _kd,
     w_branch_a, w_branch_b, w_out, norm2_g, w_up, w_down) = lp
    B, S, _ = x.shape
    ya = o_fox.reshape(B, S, D_FOX) @ w_branch_a
    yb = o_dil.reshape(B, S, D_DIL) @ w_branch_b
    mixed = jax.nn.sigmoid(gate_a) * ya + jax.nn.sigmoid(gate_b) * yb
    h = x + mixed @ w_out
    u = jax.nn.relu(rmsnorm(h, norm2_g) @ w_up)
    return h + (u * u) @ w_down

def fox_prompt(q, k, v, logf):
    B, S, H, D = q.shape
    c = jnp.cumsum(logf, axis=1).transpose(0, 2, 1)
    scale = D ** -0.5
    kpos = jnp.arange(S)

    def block(i):
        start = i * Q_BLOCK
        qb = lax.dynamic_slice_in_dim(q, start, Q_BLOCK, axis=1)
        cb = lax.dynamic_slice_in_dim(c, start, Q_BLOCK, axis=2)
        s = jnp.einsum('bqhd,bkhd->bhqk', qb, k).astype(jnp.float32) * scale
        s = s + cb[..., :, None] - c[..., None, :]
        qpos = start + jnp.arange(Q_BLOCK)
        p, _ = softmax_stats(s, kpos[None, :] <= qpos[:, None])
        return jnp.einsum('bhqk,bkhd->bqhd', p.astype(v.dtype), v)

    out = lax.map(block, jnp.arange(S // Q_BLOCK))
    return out.transpose(1, 0, 2, 3, 4).reshape(B, S, H, D)

def fox_sample(q, k_new, v_new, logf_new, k_past, v_past, logf_past):
    T = q.shape[1]
    P = k_past.shape[1]
    scale = q.shape[-1] ** -0.5
    lp = logf_past.astype(jnp.float32)
    suffix = (lax.cumsum(lp, axis=1, reverse=True) - lp).transpose(0, 2, 1)
    cnew = jnp.cumsum(logf_new, axis=1).transpose(0, 2, 1)
    s_past = jnp.einsum('bthd,bshd->bhts', q, k_past).astype(jnp.float32) * scale
    s_past = s_past + cnew[..., :, None] + suffix[..., None, :]
    s_new = jnp.einsum('bthd,bshd->bhts', q, k_new).astype(jnp.float32) * scale
    s_new = s_new + cnew[..., :, None] - cnew[..., None, :]
    ar = jnp.arange(T)
    valid = jnp.concatenate([jnp.ones((T, P), bool), ar[None, :] <= ar[:, None]], axis=-1)
    p, _ = softmax_stats(jnp.concatenate([s_past, s_new], axis=-1), valid)
    return (jnp.einsum('bhts,bshd->bthd', p[..., :P].astype(v_past.dtype), v_past)
            + jnp.einsum('bhts,bshd->bthd', p[..., P:].astype(v_new.dtype), v_new))

def band_attn(q, k, v, span):
    N, L, H, D = q.shape
    nb = -(-L // Q_BLOCK)
    Lp = nb * Q_BLOCK
    qb = jnp.pad(q, ((0, 0), (0, Lp - L), (0, 0), (0, 0))).reshape(N, nb, Q_BLOCK, H, D)
    padk = lambda t: jnp.pad(t, ((0, 0), (Q_BLOCK, Lp - L), (0, 0), (0, 0))).reshape(N, nb + 1, Q_BLOCK, H, D)
    kb, vb = padk(k), padk(v)
    kband = jnp.concatenate([kb[:, :-1], kb[:, 1:]], axis=2)
    vband = jnp.concatenate([vb[:, :-1], vb[:, 1:]], axis=2)
    qq = jnp.arange(Q_BLOCK)[:, None]
    kk = jnp.arange(2 * Q_BLOCK)[None, :]
    dist = qq + Q_BLOCK - kk
    jpos = jnp.arange(nb)[:, None, None] * Q_BLOCK - Q_BLOCK + kk[None]
    valid = (dist >= 0) & (dist <= span) & (jpos >= 0)
    s = jnp.einsum('nbqhd,nbkhd->nbhqk', qb, kband).astype(jnp.float32) * (D ** -0.5)
    p, lse = softmax_stats(s, valid[None, :, None])
    o = jnp.einsum('nbhqk,nbkhd->nbqhd', p.astype(v.dtype), vband).reshape(N, Lp, H, D)[:, :L]
    lse = lse.transpose(0, 1, 3, 2).reshape(N, Lp, H)[:, :L]
    return o, lse

def dilated_prompt(q, k, v, window, dilation):
    B, S, H, D = q.shape
    L = S // dilation
    to_res = lambda t: t.reshape(B, L, dilation, H, D).transpose(0, 2, 1, 3, 4).reshape(B * dilation, L, H, D)
    o, lse = band_attn(to_res(q), to_res(k), to_res(v), window // dilation)
    o = o.reshape(B, dilation, L, H, D).transpose(0, 2, 1, 3, 4).reshape(B, S, H, D)
    lse = lse.reshape(B, dilation, L, H).transpose(0, 2, 1, 3).reshape(B, S, H)
    return o, lse

def dilated_sample(q, k_new, v_new, buf_kv, window, dilation):
    W = buf_kv.shape[1]
    T = q.shape[1]
    span = window // dilation
    ext_k = jnp.concatenate([buf_kv[:, :, 0], k_new], axis=1)
    ext_v = jnp.concatenate([buf_kv[:, :, 1], v_new], axis=1)
    e = W + jnp.arange(T)[:, None] - dilation * jnp.arange(span + 1)[None, :]
    valid = e >= 0
    e = jnp.maximum(e, 0)
    kg, vg = ext_k[:, e], ext_v[:, e]
    s = jnp.einsum('bthd,btmhd->bthm', q, kg).astype(jnp.float32) * (q.shape[-1] ** -0.5)
    p, lse = softmax_stats(s, valid[None, :, None, :])
    o = jnp.einsum('bthm,btmhd->bthd', p.astype(vg.dtype), vg)
    keep = min(window, W + T)
    new_buf = jnp.stack([ext_k[:, W + T - keep:], ext_v[:, W + T - keep:]], axis=2)
    return o, lse, new_buf

def merge_groups(outs, lses):
    o = jnp.stack(outs, 0)
    a = jax.nn.softmax(jnp.stack(lses, 0), axis=0)
    return jnp.einsum('gbsh,gbshd->bshd', a.astype(o.dtype), o)

def setup_inputs(seed: int = 0) -> dict:
    key = jax.random.key(seed)
    ks = iter(jax.random.split(key, 32))
    nrm = lambda shape, scale=1.0: scale * jax.random.normal(next(ks), shape, jnp.float32)
    n_pages = PAST_LEN // PAGE_SIZE
    n_phys = -(-5 * DEC_BATCH * n_pages // 4)
    head_bias = jnp.linspace(FORGET_BIAS_MIN, FORGET_BIAS_MAX, N_HEADS_FOX, dtype=jnp.float32)
    inp = {}
    inp['x_prompt'] = nrm((BATCH, SEQ, D_MODEL))
    inp['x_sample'] = nrm((DEC_BATCH, DEC_SEQ, D_MODEL))
    inp['cache_fox_k'] = nrm((DEPTH, n_phys, PAGE_SIZE, N_HEADS_FOX, HEAD_DIM))
    inp['cache_fox_v'] = nrm((DEPTH, n_phys, PAGE_SIZE, N_HEADS_FOX, HEAD_DIM))
    inp['cache_fox_logf'] = jax.nn.log_sigmoid(head_bias + nrm((DEPTH, n_phys, PAGE_SIZE, N_HEADS_FOX), 0.5))
    for g, (w, _r) in enumerate(DIL_PATTERNS):
        inp['cache_win%d_kv' % (g + 1)] = nrm((DEPTH, DEC_BATCH, min(w, PAST_LEN), 2, N_HEADS_DIL, HEAD_DIM))
    inp['page_table'] = jax.random.permutation(next(ks), n_phys)[: DEC_BATCH * n_pages].reshape(
        DEC_BATCH, n_pages).astype(jnp.int32)
    inp['norm1_g'] = 1.0 + nrm((DEPTH, D_MODEL), 0.05)
    inp['w_in'] = nrm((DEPTH, D_MODEL, D_IN), D_MODEL ** -0.5)
    inp['b_forget'] = head_bias + nrm((DEPTH, N_HEADS_FOX), 0.1)
    inp['qn_fox_g'] = 1.0 + nrm((DEPTH, HEAD_DIM), 0.05)
    inp['kn_fox_g'] = 1.0 + nrm((DEPTH, HEAD_DIM), 0.05)
    inp['qn_dil_g'] = 1.0 + nrm((DEPTH, N_GROUPS, HEAD_DIM), 0.05)
    inp['kn_dil_g'] = 1.0 + nrm((DEPTH, N_GROUPS, HEAD_DIM), 0.05)
    inp['w_branch_a'] = nrm((DEPTH, D_FOX, D_MODEL), D_FOX ** -0.5)
    inp['w_branch_b'] = nrm((DEPTH, D_DIL, D_MODEL), D_DIL ** -0.5)
    inp['w_out'] = nrm((DEPTH, D_MODEL, D_MODEL), D_MODEL ** -0.5)
    inp['norm2_g'] = 1.0 + nrm((DEPTH, D_MODEL), 0.05)
    inp['w_up'] = nrm((DEPTH, D_MODEL, D_FF), D_MODEL ** -0.5)
    inp['w_down'] = nrm((DEPTH, D_FF, D_MODEL), D_FF ** -0.5)
    return inp

def reference(x_prompt, x_sample, cache_fox_k, cache_fox_v, cache_fox_logf, cache_win1_kv, cache_win2_kv,
              cache_win3_kv, page_table, norm1_g, w_in, b_forget, qn_fox_g, kn_fox_g, qn_dil_g, kn_dil_g,
              w_branch_a, w_branch_b, w_out, norm2_g, w_up, w_down):
    win_caches = (cache_win1_kv, cache_win2_kv, cache_win3_kv)
    S = x_prompt.shape[1]
    DB, T, _ = x_sample.shape
    past = page_table.shape[1] * PAGE_SIZE
    pos_p = jnp.arange(S, dtype=jnp.int32)
    pos_s = past + jnp.arange(T, dtype=jnp.int32)
    h_p, h_s = x_prompt, x_sample
    kp_l, vp_l, fp_l, ks_l, vs_l, fs_l = [], [], [], [], [], []
    winp_l = [[] for _ in DIL_PATTERNS]
    wins_l = [[] for _ in DIL_PATTERNS]
    for l in range(DEPTH):
        lp = (norm1_g[l], w_in[l], b_forget[l], qn_fox_g[l], kn_fox_g[l], qn_dil_g[l], kn_dil_g[l],
              w_branch_a[l], w_branch_b[l], w_out[l], norm2_g[l], w_up[l], w_down[l])
        q_f, k_f, v_f, logf, dil, ga, gb = project(h_p, pos_p, lp)
        o_fox = fox_prompt(q_f, k_f, v_f, logf)
        outs, lses = [], []
        for g, ((w, r), (q, k, v)) in enumerate(zip(DIL_PATTERNS, dil)):
            o, lse = dilated_prompt(q, k, v, w, r)
            outs.append(o)
            lses.append(lse)
            keep = min(w, S)
            winp_l[g].append(jnp.stack([k[:, S - keep:], v[:, S - keep:]], axis=2))
        h_p = finish(h_p, o_fox, merge_groups(outs, lses), ga, gb, lp)
        kp_l.append(k_f)
        vp_l.append(v_f)
        fp_l.append(logf)
        q_f, k_f, v_f, logf, dil, ga, gb = project(h_s, pos_s, lp)
        k_past = cache_fox_k[l][page_table].reshape(DB, past, N_HEADS_FOX, HEAD_DIM)
        v_past = cache_fox_v[l][page_table].reshape(DB, past, N_HEADS_FOX, HEAD_DIM)
        f_past = cache_fox_logf[l][page_table].reshape(DB, past, N_HEADS_FOX)
        o_fox = fox_sample(q_f, k_f, v_f, logf, k_past, v_past, f_past)
        outs, lses = [], []
        for g, ((w, r), (q, k, v)) in enumerate(zip(DIL_PATTERNS, dil)):
            o, lse, new_buf = dilated_sample(q, k, v, win_caches[g][l], w, r)
            outs.append(o)
            lses.append(lse)
            wins_l[g].append(new_buf)
        h_s = finish(h_s, o_fox, merge_groups(outs, lses), ga, gb, lp)
        ks_l.append(k_f)
        vs_l.append(v_f)
        fs_l.append(logf)
    y_prompt = h_p
    y_sample = h_s
    fox_k_prompt = jnp.stack(kp_l, 0)
    fox_v_prompt = jnp.stack(vp_l, 0)
    fox_logf_prompt = jnp.stack(fp_l, 0)
    win1_kv_prompt = jnp.stack(winp_l[0], 0)
    win2_kv_prompt = jnp.stack(winp_l[1], 0)
    win3_kv_prompt = jnp.stack(winp_l[2], 0)
    fox_k_sample = jnp.stack(ks_l, 0)
    fox_v_sample = jnp.stack(vs_l, 0)
    fox_logf_sample = jnp.stack(fs_l, 0)
    win1_kv_sample = jnp.stack(wins_l[0], 0)
    win2_kv_sample = jnp.stack(wins_l[1], 0)
    win3_kv_sample = jnp.stack(wins_l[2], 0)
    return (y_prompt, y_sample, fox_k_prompt, fox_v_prompt, fox_logf_prompt, win1_kv_prompt, win2_kv_prompt,
            win3_kv_prompt, fox_k_sample, fox_v_sample, fox_logf_sample, win1_kv_sample, win2_kv_sample,
            win3_kv_sample)


_drawn_inputs = setup_inputs


def setup_inputs(seed=0):
    import zlib

    import numpy as np

    out = dict(_drawn_inputs(seed))
    spreads = {}
    factors = {'qn_fox_g': 8.0, 'qn_dil_g': 8.0}
    for name, (base, spread) in spreads.items():
        noise = np.random.default_rng([zlib.crc32(name.encode()), seed]).standard_normal(out[name].shape)
        drawn = base * np.exp(spread * noise) if base else spread * noise
        out[name] = __import__('jax').numpy.asarray(drawn.astype(out[name].dtype))
    for name, factor in factors.items():
        out[name] = (out[name] * factor).astype(out[name].dtype)
    return out
```

```python
from contextlib import ExitStack

import numpy as np
import concourse.bass as bass
from concourse import mybir

F32 = mybir.dt.float32
F32R = mybir.dt.float32r
I32 = mybir.dt.int32
ALU = mybir.AluOpType
ACT = mybir.ActivationFunctionType
AX = mybir.AxisListType

P = 128
D_MODEL = 1024
SEQ = 512
DEC_BATCH = 8
DEC_SEQ = 8
PAST_LEN = 4096
PAGE = 128
N_PAGES = PAST_LEN // PAGE
HEADS = 8
HEAD_DIM = 64
D_HEADS = HEADS * HEAD_DIM
PAIRS = HEADS // 2
DIL = ((128, 1), (512, 4), (2048, 16))
SETS = 1 + len(DIL)
D_FF = 4 * D_MODEL
EPS = 1e-6
ROPE_THETA = 10000.0
NEG = -1.0e30

KT = D_MODEL // P
N_SAMPLE = DEC_BATCH * DEC_SEQ
N_TOK = SEQ + N_SAMPLE
TILES = SEQ // P + 1
TOK_PAD = TILES * P
HALF_TOK = N_TOK // 2
SLAB = 2048
Q_TILES = SEQ // P
HT = HEADS * DEC_SEQ
FORGET_COL = 3 * D_HEADS
DIL_COL = FORGET_COL + HEADS
GATE_COL = DIL_COL + len(DIL) * 3 * D_HEADS
D_IN = GATE_COL + 2 * D_MODEL
GATE_TILES = 2 * D_MODEL // P


def tile_rows(t):
    return P if t < Q_TILES else N_SAMPLE


def project_tokens(nc, a, sem, ident):
    with ExitStack() as ctx:
        def sb(name, shape, dt=F32):
            return ctx.enter_context(nc.sbuf_tensor(name, shape, dt))

        def ps(name, shape):
            return ctx.enter_context(nc.psum_tensor(name, shape, F32))

        x_in = sb("x_in", [P, TILES, D_MODEL])
        g1_row = sb("g1_row", [P, D_MODEL])
        x_sq = sb("x_sq", [P, D_MODEL])
        x_ss = sb("x_ss", [P, TILES])
        x_std = sb("x_std", [P, TILES])
        x_rstd = sb("x_rstd", [P, TILES])
        xn_hi = sb("xn_hi", [P, KT, TOK_PAD], F32R)
        xn_lo = sb("xn_lo", [P, KT, TOK_PAD], F32R)
        w_raw = sb("w_raw", [P, 2, SLAB])
        w_hi = sb("w_hi", [P, 2, SLAB], F32R)
        w_lo = sb("w_lo", [P, 2, SLAB], F32R)
        wf_raw = sb("wf_raw", [P, KT, P])
        wf_hi = sb("wf_hi", [P, KT, P], F32R)
        wf_lo = sb("wf_lo", [P, KT, P], F32R)
        z_t = sb("z_t", [HEADS, TOK_PAD])
        bf_row = sb("bf_row", [P, HEADS])
        lz, lz_neg, lz_e, lz_u, lz_ln, lz_d, lz_r, logf = (
            sb(n, [P, TILES, HEADS]) for n in ("lz", "lz_neg", "lz_e", "lz_u", "lz_ln", "lz_d", "lz_r", "logf"))
        rope_c = sb("rope_c", [P, SETS, TILES, HEAD_DIM])
        rope_s = sb("rope_s", [P, SETS, TILES, HEAD_DIM])
        gain = sb("gain", [P, 2, SETS, HEAD_DIM])
        rope_cg = sb("rope_cg", [P, 2, TILES, HEAD_DIM])
        rope_sg = sb("rope_sg", [P, 2, TILES, HEAD_DIM])
        y_raw, y_sq, y_unit, y_cos, y_sin = (
            sb(n, [P, 2, D_HEADS]) for n in ("y_raw", "y_sq", "y_unit", "y_cos", "y_sin"))
        y_ss, y_std, y_rstd = (sb(n, [P, 2, HEADS]) for n in ("y_ss", "y_std", "y_rstd"))
        eps_col = sb("eps_col", [P, 1])
        y_rot = sb("y_rot", [P, TILES, D_HEADS])
        y_t = sb("y_t", [P, TILES, D_HEADS])
        v_raw = sb("v_raw", [P, TILES, D_HEADS])
        gate = sb("gate", [P, 2, N_TOK])
        acc = ps("acc", [P, 5, 512])
        tp = ps("tp", [P, 2, 512])

        consts_in = sem("p1_consts_in")
        x_loaded, sample_loaded, pad_zeroed = sem("x_loaded"), sem("sample_loaded"), sem("pad_zeroed")
        x_squared, x_std_done, x_rstd_done = sem("x_squared"), sem("x_std_done"), sem("x_rstd_done")
        x_scaled, x_turned, x_hi_done, x_lo_done = sem("x_scaled"), sem("x_turned"), sem("x_hi_done"), sem("x_lo_done")
        wf_loaded, wf_hi_done, wf_lo_done = sem("wf_loaded"), sem("wf_hi_done"), sem("wf_lo_done")
        z_summed, z_copied, z_turned = sem("z_summed"), sem("z_copied"), sem("z_turned")
        lz_step, lz_exp, lz_log = sem("lz_step"), sem("lz_exp"), sem("lz_log")
        slab_loaded = [sem(f"slab_loaded{i}") for i in range(2)]
        slab_hi_done, slab_lo_done, half_used = sem("slab_hi_done"), sem("slab_lo_done"), sem("half_used")
        acc_done, acc_used = sem("acc_done"), sem("acc_used")
        raw_done, sq_done, ss_done = sem("raw_done"), sem("sq_done"), sem("ss_done")
        std_done, eps_set = sem("std_done"), sem("eps_set")
        rstd_done, unit_done, cos_done = sem("rstd_done"), sem("unit_done"), sem("cos_done")
        sin_done, rot_done, tables_done = sem("sin_done"), sem("rot_done"), sem("tables_done")
        y_turned, yt_done = sem("y_turned"), sem("yt_done")
        v_copied = sem("v_copied")
        yt_stored, rot_stored, v_stored = sem("yt_stored"), sem("rot_stored"), sem("v_stored")
        yt_free, rot_free, v_free = sem("yt_free"), sem("rot_free"), sem("v_free")
        gate_acc, gate_done, gate_free = sem("gate_acc"), sem("gate_done"), sem("gate_free")
        gate_stored = [sem(f"gate_stored{i}") for i in range(2)]
        lf_stored, window_copied = sem("lf_stored"), sem("window_copied")

        w_in = a["w_in"][0]
        N_SLABS = 6 * SETS
        N_GATE_SLABS = GATE_TILES // 2
        N_CONSTS = 16 * 9
        LZ_STEPS = 9

        def slab_source(n):
            if n < N_SLABS:
                s, j = n // 6, n % 6
                col = s * 3 * D_HEADS + (HEADS if s else 0) + (j // 2) * D_HEADS
                rows = w_in[(j % 2) * 512:(j % 2) * 512 + 512, col:col + D_HEADS]
                return rows.rearrange("(k p) n -> p k n", p=P)
            col = GATE_COL + (n - N_SLABS) * 256
            return w_in[:, col:col + 256].rearrange("(k p) n -> p k n", p=P)

        def row_target(g, t, part):
            if t == Q_TILES:
                if g < 0:
                    return (a["fox_k_sample"], a["fox_v_sample"])[part][0].rearrange("b t h d -> (b t) (h d)")
                w = DIL[g][0]
                return a["win_sample"][g][0, :, w - DEC_SEQ:w, part].rearrange("b t h d -> b t (h d)")
            if g < 0:
                return (a["fox_k_prompt"], a["fox_v_prompt"])[part][0, 0, t * P:t * P + P].rearrange("t h d -> t (h d)")
            row = t * P - (SEQ - min(DIL[g][0], SEQ))
            return a["win_prompt"][g][0, 0, row:row + P, part].rearrange("t h d -> t (h d)") if row >= 0 else None

        def kept_tiles(g):
            return TILES if g < 0 else min(DIL[g][0], SEQ) // P + 1

        window_copies = []
        for g, parts in ((2, 4), (1, 1)):
            step = (DIL[g][0] - DEC_SEQ) // parts
            for b in range(DEC_BATCH):
                for r in range(0, DIL[g][0] - DEC_SEQ, step):
                    window_copies.append((a["win_sample"][g][0, b, r:r + step], a["windows"][g][0, b, r + DEC_SEQ:r + DEC_SEQ + step]))
        for b in range(DEC_BATCH):
            window_copies.append((a["win_sample"][0][0, b, 0:DIL[0][0] - DEC_SEQ], a["windows"][0][0, b, DEC_SEQ:DIL[0][0]]))

        block = ctx.enter_context(nc.Block())

        @block.sync
        def _(sp):
            copies = [0]

            def copy_window():
                if copies[0] < len(window_copies):
                    dst, src = window_copies[copies[0]]
                    copies[0] += 1
                    sp.dma_start(dst.rearrange("r k h d -> r (k h d)"), src.rearrange("r k h d -> r (k h d)")).then_inc(window_copied, 16)

            def load_slab(n):
                if n >= N_SLABS + N_GATE_SLABS:
                    return
                if n >= 2:
                    sp.wait_ge(slab_lo_done, n - 1)
                k = 4 if n < N_SLABS else 8
                sp.dma_start(w_raw[:, n % 2, :].rearrange("p (k n) -> p k n", k=k), slab_source(n)).then_inc(slab_loaded[n % 2], 16)

            sp.dma_start(x_in[:, 0:Q_TILES, :], a["x_prompt"][0].rearrange("(t p) d -> p t d", p=P)).then_inc(x_loaded, 16)
            sp.dma_start(x_in[0:N_SAMPLE, Q_TILES, :], a["x_sample"].rearrange("b t d -> (b t) d")).then_inc(sample_loaded, 16)
            sp.dma_start(g1_row[:], a["norm1_g"][0].partition_broadcast(P)).then_inc(consts_in, 16)
            sp.dma_start(ident[:], a["c_ident"]).then_inc(consts_in, 16)
            sp.dma_start(wf_raw[:], w_in[:, FORGET_COL:FORGET_COL + P].rearrange("(k p) n -> p k n", p=P)).then_inc(wf_loaded, 16)
            load_slab(0)
            load_slab(1)
            sp.dma_start(bf_row[:], a["b_forget"][0].partition_broadcast(P)).then_inc(consts_in, 16)
            sp.dma_start(rope_c[:], a["c_cos"]).then_inc(consts_in, 16)
            sp.dma_start(rope_s[:], a["c_sin"]).then_inc(consts_in, 16)
            for i, (first, rest) in enumerate(((a["qn_fox_g"], a["qn_dil_g"]), (a["kn_fox_g"], a["kn_dil_g"]))):
                sp.dma_start(gain[:, i, 0, :], first[0].partition_broadcast(P)).then_inc(consts_in, 16)
                sp.dma_start(gain[:, i, 1:SETS, :], rest[0].partition_broadcast(P)).then_inc(consts_in, 16)
            sp.wait_ge(lz_step, LZ_STEPS)
            sp.dma_start(a["lf_s"].rearrange("(t p) h -> p t h", p=P), logf[:]).then_inc(lf_stored, 16)
            sp.dma_start(a["fox_logf_prompt"][0, 0].rearrange("(t p) h -> p t h", p=P), logf[:, 0:Q_TILES, :]).then_inc(lf_stored, 16)
            sp.dma_start(a["fox_logf_sample"][0].rearrange("b t h -> (b t) h"), logf[0:N_SAMPLE, Q_TILES, :]).then_inc(lf_stored, 16)
            n_rot = n_v = 0
            sp.sem_inc(rot_free, 1)
            sp.sem_inc(v_free, 1)
            sp.sem_inc(yt_free, 1)
            for s in range(SETS):
                g = s - 1
                for c in range(3):
                    load_slab(6 * s + 2 * c + 2)
                    copy_window()
                    load_slab(6 * s + 2 * c + 3)
                    copy_window()
                    if s and c == 0:
                        sp.wait_ge(rot_stored, 16 * n_rot)
                        sp.sem_inc(rot_free, 1)
                        sp.wait_ge(v_stored, 16 * n_v)
                        sp.sem_inc(v_free, 1)
                    if c:
                        for t in range(TILES):
                            sp.wait_ge(yt_done, 10 * s + 5 * (c - 1) + t + 3)
                            dst = (a["qt_s"], a["kt_s"])[c - 1][s, :, :, t * P:t * P + P].rearrange("q p n -> p q n")
                            sp.dma_start(dst, y_t[:, t, :].rearrange("p (q n) -> p q n", q=PAIRS)).then_inc(yt_stored, 16)
                        sp.wait_ge(yt_stored, 16 * 5 * (2 * s + c))
                        sp.sem_inc(yt_free, 1)
                    for t in range(TILES):
                        if c == 1 and (dst := row_target(g, t, 0)) is not None:
                            sp.wait_ge(rot_done, 10 * s + 5 + t + 1)
                            sp.dma_start(dst, y_rot[0:tile_rows(t), t, :]).then_inc(rot_stored, 16)
                            n_rot += 1
                        if c == 2:
                            sp.wait_ge(v_copied, 5 * s + t + 1)
                            src = v_raw[0:tile_rows(t), t, :]
                            sp.dma_start(a["v_s"][s, t * P:t * P + tile_rows(t)], src).then_inc(v_stored, 16)
                            n_v += 1
                            if (dst := row_target(g, t, 1)) is not None:
                                sp.dma_start(dst, src).then_inc(v_stored, 16)
                                n_v += 1
            sp.sem_inc(gate_free, 1)
            for i in range(N_GATE_SLABS):
                load_slab(N_SLABS + i + 2)
                copy_window()
                copy_window()
                for f in (2 * i, 2 * i + 1):
                    sp.wait_ge(gate_done, f + 3)
                    sp.dma_start(a["gate_s"][f], gate[:, f % 2, :]).then_inc(gate_stored[f % 2], 16)
                    if f:
                        sp.wait_ge(gate_stored[(f - 1) % 2], 16 * ((f - 1) // 2 + 1))
                    sp.sem_inc(gate_free, 1)
            while copies[0] < len(window_copies):
                copy_window()
            sp.wait_ge(lf_stored, 48)
            sp.wait_ge(rot_stored, 16 * n_rot)
            sp.wait_ge(v_stored, 16 * n_v)
            sp.wait_ge(yt_stored, 16 * 10 * SETS)
            for i in range(2):
                sp.wait_ge(gate_stored[i], 16 * GATE_TILES // 2)
            sp.wait_ge(window_copied, 16 * len(window_copies))

        @block.gpsimd
        def _(gp):
            gp.memset(xn_hi[:, :, N_TOK:].bitcast(F32), 0.0).then_inc(pad_zeroed, 1)
            gp.memset(xn_lo[:, :, N_TOK:].bitcast(F32), 0.0).then_inc(pad_zeroed, 1)
            gp.wait_ge(pad_zeroed, 2)
            gp.memset(z_t[:, N_TOK:], 0.0).then_inc(pad_zeroed, 1)
            gp.wait_ge(pad_zeroed, 3)
            gp.memset(x_in[N_SAMPLE:, Q_TILES, :], 0.0).then_inc(pad_zeroed, 1)
            gp.wait_ge(pad_zeroed, 4)
            with gp.Fori(0, SETS) as s:
                gp.wait_ge(tables_done, 6 * s + 6)
                gp.wait_ge(rot_free, s + 1)
                for c in range(2):
                    for t in range(TILES):
                        slot, at = (5 * c + t) % 2, 10 * s + 5 * c + t
                        heads = [z[:, slot, :].rearrange("p (h d) -> p h d", h=HEADS) for z in (y_unit, y_cos)]
                        gp.wait_ge(unit_done, at + 3)
                        gp.tensor_tensor(heads[1], heads[0], rope_cg[:, c, t, :].unsqueeze(1).to_broadcast([P, HEADS, HEAD_DIM]),
                                         ALU.mult).then_inc(cos_done, 1)
                        gp.wait_ge(cos_done, at + 1)
                        gp.wait_ge(sin_done, at + 1)
                        gp.wait_ge(y_turned, at + 1)
                        gp.tensor_tensor(y_rot[:, t, :], y_cos[:, slot, :], y_sin[:, slot, :], ALU.add).then_inc(rot_done, 1)

        @block.scalar
        def _(act):
            def split_hi(rounds, slot):
                act.wait_ge(slab_loaded[slot], 16 * rounds)
                act.activation(w_hi[:, slot, :], w_raw[:, slot, :], ACT.Copy).then_inc(slab_hi_done, 1)

            act.wait_ge(x_loaded, 16)
            for t in range(TILES):
                if t == Q_TILES:
                    act.wait_ge(sample_loaded, 16)
                    act.wait_ge(pad_zeroed, 4)
                if t:
                    act.wait_ge(x_squared, t)
                act.activation(x_sq[:], x_in[:, t, :], ACT.Square, accum_out=x_ss[:, t:t + 1]).then_inc(x_squared, 1)
            act.wait_ge(x_squared, TILES)
            act.wait_ge(eps_set, 1)
            act.activation(x_std[:], x_ss[:], ACT.Sqrt, scale=1.0 / D_MODEL, bias=eps_col[:]).then_inc(x_std_done, 1)
            act.wait_ge(wf_loaded, 16)
            act.activation(wf_hi[:], wf_raw[:], ACT.Copy).then_inc(wf_hi_done, 1)
            split_hi(1, 0)
            for u in range(2 * TILES):
                t, half = u // 2, u % 2
                r = tile_rows(t)
                act.wait_ge(x_turned, u + 1)
                act.activation(xn_hi[:, 4 * half:4 * half + 4, t * P:t * P + r],
                               tp[:, u % 2, :].rearrange("p (k n) -> p k n", k=4)[:, :, 0:r], ACT.Copy).then_inc(x_hi_done, 1)
            split_hi(1, 1)
            act.wait_ge(z_summed, 1)
            for h in range(2):
                act.activation(z_t[:, h * HALF_TOK:(h + 1) * HALF_TOK], acc[0:HEADS, h, 0:HALF_TOK], ACT.Copy).then_inc(z_copied, 1)
            act.wait_ge(lz_step, 2)
            act.activation(lz_e[:], lz_neg[:], ACT.Exp).then_inc(lz_exp, 1)
            act.wait_ge(lz_step, 3)
            act.activation(lz_ln[:], lz_u[:], ACT.Ln).then_inc(lz_log, 1)

            def turned_rows(s, c):
                act.wait_ge(yt_free, 2 * s + c + 1)
                for t in range(TILES):
                    slot, at = (5 * c + t) % 2, 10 * s + 5 * c + t
                    act.wait_ge(y_turned, at + 6)
                    act.activation(y_t[:, t, :], tp[:, slot, :], ACT.Copy).then_inc(yt_done, 1)

            with act.Fori(0, SETS) as s:
                for c in range(3):
                    act.wait_ge(half_used, 3 * s + c + 1)
                    split_hi(3 * s + c + 2, 0)
                    if c:
                        turned_rows(s, c - 1)
                    for t in range(TILES):
                        act.wait_ge(acc_done, 15 * s + 5 * c + t + 1)
                        if c == 2:
                            if t == 0:
                                act.wait_ge(v_free, s + 1)
                            act.activation(v_raw[:, t, :], acc[:, t, :], ACT.Copy).then_inc(v_copied, 1)
                            act.wait_ge(v_copied, 5 * s + t + 1)
                            act.sem_inc(acc_used, 1)
                            continue
                        slot, at = (5 * c + t) % 2, 10 * s + 5 * c + t
                        act.wait_ge(unit_done, at + 1)
                        act.activation(y_raw[:, slot, :], acc[:, t, :], ACT.Copy).then_inc(raw_done, 1)
                        act.wait_ge(raw_done, at + 1)
                        act.sem_inc(acc_used, 1)
                        act.activation(y_sq[:, slot, :], y_raw[:, slot, :], ACT.Square).then_inc(sq_done, 1)
                        act.wait_ge(ss_done, at + 1)
                        act.activation(y_std[:, slot, :], y_ss[:, slot, :], ACT.Sqrt, scale=1.0 / HEAD_DIM, bias=eps_col[:]).then_inc(std_done, 1)
                    split_hi(3 * s + c + 2, 1)
            for f in range(GATE_TILES):
                act.wait_ge(gate_acc, f + 1)
                act.wait_ge(gate_free, f + 1)
                for h in range(2):
                    last = act.activation(gate[:, f % 2, h * HALF_TOK:(h + 1) * HALF_TOK], acc[:, 2 * (f % 2) + h, 0:HALF_TOK], ACT.Sigmoid)
                last.then_inc(gate_done, 1)
                if f % 2 and N_SLABS + f // 2 + 2 < N_SLABS + N_GATE_SLABS:
                    split_hi((N_SLABS + f // 2 + 2) // 2 + 1, (f // 2) % 2)

        @block.vector
        def _(ve):
            def split_lo(n, slot):
                ve.wait_ge(slab_hi_done, n + 1)
                ve.tensor_tensor(w_lo[:, slot, :], w_raw[:, slot, :], w_hi[:, slot, :].bitcast(F32), ALU.subtract).then_inc(slab_lo_done, 1)

            ve.memset(eps_col[:], EPS).then_inc(eps_set, 1)
            ve.sem_inc(unit_done, 2)
            ve.wait_ge(consts_in, N_CONSTS)
            ve.wait_ge(x_std_done, 1)
            ve.reciprocal(x_rstd[:], x_std[:]).then_inc(x_rstd_done, 1)
            ve.wait_ge(x_rstd_done, 1)
            for t in range(TILES):
                ve.scalar_tensor_tensor(out=x_in[:, t, :], in0=x_in[:, t, :], scalar=x_rstd[:, t:t + 1], in1=g1_row[:],
                                        op0=ALU.mult, op1=ALU.mult).then_inc(x_scaled, 1)
            ve.wait_ge(wf_hi_done, 1)
            ve.tensor_tensor(wf_lo[:], wf_raw[:], wf_hi[:].bitcast(F32), ALU.subtract).then_inc(wf_lo_done, 1)
            split_lo(0, 0)
            for u in range(2 * TILES):
                t, half = u // 2, u % 2
                r = tile_rows(t)
                ve.wait_ge(x_hi_done, u + 1)
                part = (slice(None), slice(4 * half, 4 * half + 4), slice(t * P, t * P + r))
                ve.tensor_tensor(xn_lo[part], tp[:, u % 2, :].rearrange("p (k n) -> p k n", k=4)[:, :, 0:r],
                                 xn_hi[part].bitcast(F32), ALU.subtract).then_inc(x_lo_done, 1)
            split_lo(1, 1)

            ve.wait_ge(z_turned, 1)
            ve.tensor_tensor(lz[:], tp[:, 0, 0:TILES * HEADS].rearrange("p (t h) -> p t h", t=TILES),
                             bf_row[:].unsqueeze(1).to_broadcast([P, TILES, HEADS]), ALU.add).then_inc(lz_step, 1)
            ve.wait_ge(lz_step, 1)
            ve.scalar_tensor_tensor(out=lz_neg[:], in0=lz[:], scalar=-1.0, in1=lz[:], op0=ALU.mult, op1=ALU.min).then_inc(lz_step, 1)
            ve.wait_ge(lz_exp, 1)
            ve.tensor_scalar(lz_u[:], lz_e[:], 1.0, None, ALU.add).then_inc(lz_step, 1)
            ve.wait_ge(lz_step, 3)
            ve.scalar_tensor_tensor(out=lz_d[:], in0=lz_u[:], scalar=-1.0, in1=lz_e[:], op0=ALU.add, op1=ALU.subtract).then_inc(lz_step, 1)
            ve.reciprocal(lz_r[:], lz_u[:]).then_inc(lz_step, 1)
            ve.wait_ge(lz_step, 5)
            ve.tensor_tensor(lz_d[:], lz_d[:], lz_r[:], ALU.mult).then_inc(lz_step, 1)
            ve.tensor_scalar(lz[:], lz[:], 0.0, None, ALU.min).then_inc(lz_step, 1)
            ve.wait_ge(lz_step, 7)
            ve.wait_ge(lz_log, 1)
            ve.tensor_tensor(lz_d[:], lz_d[:], lz_ln[:], ALU.subtract).then_inc(lz_step, 1)
            ve.wait_ge(lz_step, 8)
            ve.tensor_tensor(logf[:], lz[:], lz_d[:], ALU.add).then_inc(lz_step, 1)

            with ve.Fori(0, SETS) as s:
                for c in range(2):
                    scale = (float(HEAD_DIM) ** -0.5, 1.0)[c]
                    H = HEAD_DIM // 2
                    cos, sin = (x[:, bass.ds(s, 1), :, :].rearrange("p a t d -> p (a t) d") for x in (rope_c, rope_s))
                    gr = gain[:, c, bass.ds(s, 1), :]
                    for out, table, lo, glo, w in ((rope_cg, cos, 0, 0, HEAD_DIM), (rope_sg, sin, 0, H, H), (rope_sg, sin, H, 0, H)):
                        ve.scalar_tensor_tensor(out=out[:, c, :, lo:lo + w], in0=table[:, :, lo:lo + w], scalar=scale,
                                                in1=gr[:, :, glo:glo + w].to_broadcast([P, TILES, w]),
                                                op0=ALU.mult, op1=ALU.mult).then_inc(tables_done, 1)
                ve.wait_ge(tables_done, 6 * s + 6)
                for c in range(3):
                    split_lo(6 * s + 2 * c + 2, 0)
                    for t in range(TILES):
                        if c == 2:
                            break
                        slot, at = (5 * c + t) % 2, 10 * s + 5 * c + t
                        raw, sq, unit, sn = (z[:, slot, :].rearrange("p (h d) -> p h d", h=HEADS) for z in (y_raw, y_sq, y_unit, y_sin))
                        ve.wait_ge(sq_done, at + 1)
                        ve.tensor_reduce(y_ss[:, slot, :], sq, AX.X, ALU.add).then_inc(ss_done, 1)
                        ve.wait_ge(std_done, at + 1)
                        ve.reciprocal(y_rstd[:, slot, :], y_std[:, slot, :]).then_inc(rstd_done, 1)
                        ve.wait_ge(rstd_done, at + 1)
                        ve.tensor_tensor(unit, raw, y_rstd[:, slot, :].unsqueeze(2).to_broadcast([P, HEADS, HEAD_DIM]),
                                         ALU.mult).then_inc(unit_done, 1)
                        ve.wait_ge(unit_done, at + 3)
                        ve.wait_ge(cos_done, at + 1)
                        H = HEAD_DIM // 2
                        for lo, other in ((0, H), (H, 0)):
                            last = ve.tensor_tensor(sn[:, :, lo:lo + H], unit[:, :, other:other + H],
                                                    rope_sg[:, c, t, lo:lo + H].unsqueeze(1).to_broadcast([P, HEADS, H]), ALU.mult)
                        last.then_inc(sin_done, 1)
                    split_lo(6 * s + 2 * c + 3, 1)
            for i in range(N_GATE_SLABS - 2):
                split_lo(N_SLABS + i + 2, i % 2)

        @block.tensor
        def _(pe):
            pe.sem_inc(acc_used, 5)
            pe.sem_inc(y_turned, 5)
            pe.sem_inc(yt_done, 2)
            pe.sem_inc(gate_done, 2)
            for u in range(2 * TILES):
                t, half = u // 2, u % 2
                pe.wait_ge(x_scaled, t + 1)
                if u >= 2:
                    pe.wait_ge(x_lo_done, u - 1)
                for k in range(4):
                    last = pe.transpose(tp[:, u % 2, k * P:k * P + P], x_in[:, t, (4 * half + k) * P:(4 * half + k + 1) * P], ident[:])
                last.then_inc(x_turned, 1)
            pe.wait_ge(wf_lo_done, 1)
            pe.wait_ge(x_lo_done, 2 * TILES)
            pe.wait_ge(pad_zeroed, 4)
            for h in range(2):
                for k in range(KT):
                    for i, (w, x) in enumerate(((wf_hi, xn_hi), (wf_lo, xn_hi), (wf_hi, xn_lo))):
                        last = pe.matmul(acc[:, h, 0:HALF_TOK], w[:, k, :], x[:, k, h * HALF_TOK:(h + 1) * HALF_TOK],
                                         start=(k == 0 and i == 0), stop=(k == KT - 1 and i == 2))
            last.then_inc(z_summed, 1)
            pe.wait_ge(z_copied, 2)
            for t in range(TILES):
                last = pe.transpose(tp[:, 0, t * HEADS:(t + 1) * HEADS], z_t[:, t * P:t * P + P], ident[0:HEADS, 0:HEADS])
            last.then_inc(z_turned, 1)
            pe.wait_ge(lz_step, 1)

            def half_chunk(s, c, half):
                slot = half
                pe.wait_ge(slab_lo_done, 6 * s + 2 * c + half + 1)
                w_parts = [w[:, slot, :].rearrange("p (k n) -> p k n", k=4) for w in (w_hi, w_lo)]
                for t in range(TILES):
                    if half == 0:
                        pe.wait_ge(acc_used, 15 * s + 5 * c + t + 1)
                    for k in range(4):
                        kk = 4 * half + k
                        for i, (x, w) in enumerate(((xn_hi, w_parts[0]), (xn_hi, w_parts[1]), (xn_lo, w_parts[0]))):
                            last = pe.matmul(acc[:, t, :], x[:, kk, t * P:t * P + P], w[:, k, :],
                                             start=(kk == 0 and i == 0), stop=(kk == KT - 1 and i == 2))
                    if half == 1:
                        last.then_inc(acc_done, 1)
                    elif t == TILES - 1:
                        last.then_inc(half_used, 1)

            def turn(s, c):
                for t in range(TILES):
                    slot, at = (5 * c + t) % 2, 10 * s + 5 * c + t
                    pe.wait_ge(rot_done, at + 1)
                    pe.wait_ge(yt_done, at + 1)
                    for q in range(PAIRS):
                        last = pe.transpose(tp[:, slot, q * P:q * P + P], y_rot[:, t, q * P:q * P + P], ident[:])
                    last.then_inc(y_turned, 1)

            with pe.Fori(0, SETS) as s:
                for c in range(3):
                    half_chunk(s, c, 0)
                    if c:
                        turn(s, c - 1)
                    half_chunk(s, c, 1)
            pe.wait_ge(acc_used, 5 + 15 * SETS)
            for f in range(GATE_TILES):
                slot = (f // 2) % 2
                if f % 2 == 0:
                    pe.wait_ge(slab_lo_done, N_SLABS + f // 2 + 1)
                pe.wait_ge(gate_done, f + 1)
                w_parts = [w[:, slot, :].rearrange("p (k n) -> p k n", k=KT)[:, :, (f % 2) * P:(f % 2) * P + P] for w in (w_hi, w_lo)]
                for k in range(KT):
                    for i, (w, x) in enumerate(((w_parts[0], xn_hi), (w_parts[1], xn_hi), (w_parts[0], xn_lo))):
                        for h in range(2):
                            last = pe.matmul(acc[:, 2 * (f % 2) + h, 0:HALF_TOK], w[:, k, :], x[:, k, h * HALF_TOK:(h + 1) * HALF_TOK],
                                             start=(k == 0 and i == 0), stop=(k == KT - 1 and i == 2))
                last.then_inc(gate_acc, 1)



FOX, WIN = 0, 1
GROUP = 2 * P
N_GROUPS = (N_PAGES // 2, 7)
PER_BATCH = sum(N_GROUPS)
WIN_GROUPS = [(0, 0, 1)] + [(1, r, 2) for r in (0, 2)] + [(2, r, 2) for r in (0, 2, 4, 6)]
WIN_COLS = sum(n for _, _, n in WIN_GROUPS) * P
WIN_NEW = len(DIL) * DEC_SEQ
FOX_RING, WIN_RING = 4, 3


def group_index(kind, b, j):
    return b * PER_BATCH + (N_GROUPS[FOX] if kind == WIN else 0) + j


def group_before(kind, b, j):
    return group_index(kind, b, j) - (1 if kind == FOX and j == 0 else 2)


def group_tiles(kind, j):
    return 2 if kind == FOX else WIN_GROUPS[j][2]


def group_new(kind, j):
    if kind == FOX:
        return 0 if j == N_GROUPS[FOX] - 1 else None
    last = j == N_GROUPS[WIN] - 1 or WIN_GROUPS[j + 1][0] != WIN_GROUPS[j][0]
    return WIN_GROUPS[j][0] if last else None


def group_set(kind, j):
    return 0 if kind == FOX else 1 + WIN_GROUPS[j][0]


def group_col(kind, j):
    return j * GROUP if kind == FOX else sum(n for _, _, n in WIN_GROUPS[:j]) * P


def segment(k_kind):
    v_kind = 1 - k_kind
    nk, nv = N_GROUPS[k_kind], N_GROUPS[v_kind]
    lead, tail = 2, 3
    steps = [("K", k_kind, j) for j in range(lead)]
    k = lead
    for j in range(nv):
        steps.append(("V", v_kind, j))
        until = lead + (nk - lead - tail) * (j + 1) // nv
        while k < until:
            steps.append(("K", k_kind, k))
            k += 1
    while k < nk:
        if k == nk - 1:
            steps.append(("F", v_kind, 0))
        steps.append(("K", k_kind, k))
        k += 1
    return steps


def keys_only():
    return [("K", FOX, j) for j in range(N_GROUPS[FOX])]


def values_only():
    return [("V", WIN, j) for j in range(N_GROUPS[WIN])] + [("-", WIN, 0)] * 2 + [("F", WIN, 0)]


def in_order(steps, stages):
    for n in range(len(steps) + max(stages.values())):
        for stage, behind in stages.items():
            if 0 <= n - behind < len(steps):
                stage(*steps[n - behind])


def attend_sample(nc, a, sem, ident):
    with ExitStack() as ctx:
        def sb(name, shape, dt=F32):
            return ctx.enter_context(nc.sbuf_tensor(name, shape, dt))

        def ps(name, shape):
            return ctx.enter_context(nc.psum_tensor(name, shape, F32))

        QS = 576
        LF_GROUPS = DEC_BATCH * N_PAGES // P
        pages = sb("pages", [1, DEC_BATCH * N_PAGES], I32)
        page_col = sb("page_col", [P, LF_GROUPS], I32)
        tri = sb("tri", [P, P])
        ones = sb("ones", [P, P])
        later = sb("later", [P, P])
        sfx = sb("sfx", [P, DEC_BATCH, N_PAGES, 2, HEADS], F32R)
        sfx_wide = sb("sfx_wide", [P, 2, 2, 2 * HT], F32R)
        lfn_wide = sb("lfn_wide", [N_SAMPLE, 2 * HT], F32R)
        lfn_raw = sb("lfn_raw", [N_SAMPLE, HEADS])
        lfn = sb("lfn", [N_SAMPLE, 2, HEADS], F32R)
        new_tri_raw = sb("new_tri_raw", [N_SAMPLE, N_SAMPLE])
        new_tri = sb("new_tri", [N_SAMPLE, N_SAMPLE], F32R)
        shift = sb("shift", [P, 3 * P], F32R)
        shift_raw = sb("shift_raw", [P, 3 * P])
        mask = sb("mask", [HT, WIN_COLS + WIN_NEW])
        mask_new = sb("mask_new", [HT, DEC_SEQ])
        qn_raw = sb("qn_raw", [P, SETS, PAIRS, N_SAMPLE])
        kn_raw = sb("kn_raw", [P, SETS, PAIRS, N_SAMPLE])
        qn_hi, qn_lo, kn_hi, kn_lo = (sb(n, [P, SETS, PAIRS, N_SAMPLE], F32R) for n in ("qn_hi", "qn_lo", "kn_hi", "kn_lo"))
        q_st = sb("q_st", [P, SETS, QS], F32R)
        k_fox = sb("k_fox", [P, FOX_RING, 2, D_HEADS])
        v_fox = sb("v_fox", [P, FOX_RING, 2, D_HEADS])
        k_win = sb("k_win", [P, WIN_RING, 2, D_HEADS])
        v_win = sb("v_win", [P, WIN_RING, 2, D_HEADS])
        spare = v_fox[:].rearrange("p a b n -> p (a b n)")
        lf_t, lf_later = (spare[:, i:i + HEADS * LF_GROUPS * P].rearrange("p (h g n) -> p h g n", h=HEADS, g=LF_GROUPS)
                          for i in (0, HEADS * LF_GROUPS * P))
        lf_rows = v_win[:].rearrange("p a b n -> p (a b n)")[:, 0:LF_GROUPS * PAGE * HEADS].rearrange("p (g n) -> p g n", g=LF_GROUPS)
        kt_hi = sb("kt_hi", [P, 2, PAIRS, GROUP + DEC_SEQ], F32R)
        kt_lo = sb("kt_lo", [P, 2, PAIRS, GROUP + DEC_SEQ], F32R)
        vv_hi = sb("vv_hi", [P, 2, 2, D_HEADS], F32R)
        vv_lo = sb("vv_lo", [P, 2, 2, D_HEADS], F32R)
        s_tmp = sb("s_tmp", [HT, 2, GROUP + DEC_SEQ])
        s_fox = sb("s_fox", [HT, PAST_LEN + DEC_SEQ])
        s_win = sb("s_win", [HT, WIN_COLS + WIN_NEW])
        mx_parts = sb("mx_parts", [HT, 2, N_GROUPS[FOX] + 1])
        mx = sb("mx", [HT, 2])
        neg_mx = sb("neg_mx", [HT, 2])
        den_parts = sb("den_parts", [HT, 2, N_GROUPS[FOX] + 1])
        den = sb("den", [HT, 2])
        r_den = sb("r_den", [HT, 2])
        prob = sb("prob", [HT, 2, GROUP])
        prob_new = sb("prob_new", [HT, 2, WIN_NEW])
        pt = sb("pt", [P, 2, 2, 2, HT], F32R)
        ptn = sb("ptn", [WIN_NEW, 2, 2, HT], F32R)
        vn_raw = sb("vn_raw", [WIN_NEW, 2, D_HEADS])
        vn_hi = sb("vn_hi", [WIN_NEW, 2, D_HEADS], F32R)
        vn_lo = sb("vn_lo", [WIN_NEW, 2, D_HEADS], F32R)
        o_low = sb("o_low", [HT, D_HEADS])
        o_rows = sb("o_rows", [HT, D_HEADS])
        o_t = sb("o_t", [P, 2, PAIRS, N_SAMPLE])
        ktp = ps("ktp", [P, 2, PAIRS, GROUP])
        s_ps = ps("s_ps", [P, 2, 512])
        pt_ps = ps("pt_ps", [P, 512])
        o_ps = ps("o_ps", [P, 512])

        raw = {("K", FOX): k_fox, ("V", FOX): v_fox, ("K", WIN): k_win, ("V", WIN): v_win}
        scores = (s_fox, s_win)
        new_rows = (DEC_SEQ, WIN_NEW)
        main_cols = (PAST_LEN, WIN_COLS)

        in_small, lf_gathered, idx_in = sem("p2_small_in"), sem("lf_gathered"), sem("idx_in")
        zeroed, parts_hi, parts_lo = sem("q_zeroed"), sem("p2_parts_hi"), sem("p2_parts_lo")
        lf_turned, lf_copied, sfx_summed, sfx_hi, sfx_lo = (sem(n) for n in ("lf_turned", "lf_copied", "sfx_summed", "sfx_hi", "sfx_lo"))
        q_ready = (sem("q_fox_ready"), sem("q_win_ready"))
        loaded = {(w, FOX): [sem(f"{w}_fox_in{i}") for i in range(FOX_RING)] for w in "KV"} | \
                 {(w, WIN): [sem(f"{w}_win_in{i}") for i in range(WIN_RING)] for w in "KV"}
        N_SMALL = 16 * (9 + 2 * SETS)
        names = ("k_turned", "k_hi", "k_lo", "k_scored", "s_done",
                 "v_hi", "v_lo", "p_done", "p_turned", "p_hi", "p_lo", "v_summed")
        g = {n: sem(n) for n in names}
        tmp_fox, tmp_win = sem("s_tmp_fox"), sem("s_tmp_win")
        mx_done, mx_neg = (sem("mx_fox"), sem("mx_win")), (sem("neg_fox"), sem("neg_win"))
        s_new_tmp, s_new_done = sem("s_new_tmp"), sem("s_new_done")
        vn_in = (sem("vn_fox_in"), sem("vn_win_in"))
        den_done, r_den_done, o_low_done, o_sum_done, o_done, o_turned, o_out = (
            sem(n) for n in ("den_done", "r_den_done", "o_low_done", "o_sum_done", "o_done", "o_turned", "o_diag"))
        vn_split = sem("vn_split")
        o_stored, sfx_laid, lfn_laid = sem("o_stored"), sem("sfx_laid"), sem("lfn_laid")

        SETUP_PARTS = 5

        def raw_arrived(eng, what, kind, b, j):
            ring = FOX_RING if kind == FOX else WIN_RING
            slot, n = j % ring, N_GROUPS[kind]
            each = len([i for i in range(n) if i % ring == slot])
            pieces = 2 if kind == FOX else 1
            eng.wait_ge(loaded[what, kind][slot], 16 * pieces * (each * b + j // ring + 1))

        def raw_group(what, kind, j):
            return raw[what, kind][:, j % (FOX_RING if kind == FOX else WIN_RING), 0:group_tiles(kind, j), :]

        held = sem("held")

        def hold(eng):
            eng.sem_inc(held, 1)

        def done(eng, s, index):
            eng.wait_ge(s, index + 1 + PER_BATCH)

        block = ctx.enter_context(nc.Block())

        @block.sync
        def _(sp):
            small = [(pages[:], a["page_table"].rearrange("b n -> (b n)").unsqueeze(0)), (tri[:], a["c_tri"]), (ones[:], a["c_ones"]),
                     (later[:], a["c_later"]), (shift_raw[:], a["c_shift"]), (mask[:], a["c_mask_win"]), (mask_new[:], a["c_mask_new"]),
                     (new_tri_raw[:], a["c_new_tri"]), (lfn_raw[:], a["lf_s"][SEQ:N_TOK])]
            for s in range(SETS):
                small.append((qn_raw[:, s], a["qt_s"][s, :, :, SEQ:N_TOK].rearrange("q p n -> p q n")))
                small.append((kn_raw[:, s], a["kt_s"][s, :, :, SEQ:N_TOK].rearrange("q p n -> p q n")))
            for dst, src in small:
                sp.dma_start(dst, src).then_inc(in_small, 16)
            sp.wait_ge(in_small, N_SMALL)

            def load(what, kind, b, j):
                ring = FOX_RING if kind == FOX else WIN_RING
                slot, n = j % ring, N_GROUPS[kind]
                gone = j - ring if j >= ring else max(i for i in range(n) if i % ring == slot) - PER_BATCH
                done(sp, g["k_turned"] if what == "K" else g["v_lo"], group_index(kind, b, 0) + gone)
                dst, arrived = raw[what, kind][:, slot], loaded[what, kind][slot]
                if kind == FOX:
                    cache = a["cache_fox_k"] if what == "K" else a["cache_fox_v"]
                    for i in range(2):
                        page = sp.value_load(pages[0:1, bass.ds(b * N_PAGES + 2 * j + i, 1)], min_val=0, max_val=cache.shape[1] - 1)
                        sp.dma_start(dst[:, i, :], cache[0, bass.ds(page, 1)].rearrange("a p h d -> p (a h d)")).then_inc(arrived, 16)
                    return
                w, r, tiles = WIN_GROUPS[j]
                rows = a["windows"][w][0, bass.ds(b, 1)].rearrange("a (m r) k h d -> m (a r) k (h d)", r=DIL[w][1])
                sp.dma_start(dst[:, 0:tiles, :], rows[:, r:r + tiles, 0 if what == "K" else 1, :]).then_inc(arrived, 16)

            def load_new(kind, b):
                done(sp, g["v_lo"], group_index(kind, b, N_GROUPS[kind] - 1) - PER_BATCH)
                for i in range(1 if kind == FOX else len(DIL)):
                    src = a["v_s"][i + kind, bass.ds(SEQ + b * DEC_SEQ, DEC_SEQ)]
                    sp.dma_start(vn_raw[i * DEC_SEQ:(i + 1) * DEC_SEQ, kind, :], src).then_inc(vn_in[kind], 16)

            def steps(seg, b_keys, b_values):
                for what, kind, j in seg:
                    if what == "K":
                        load("K", kind, b_keys, j)
                    elif what == "V":
                        if j == 0:
                            load_new(kind, b_values)
                        load("V", kind, b_values, j)

            steps(keys_only(), 0, None)
            sp.wait_ge(sfx_summed, 1)
            with sp.Fori(0, DEC_BATCH - 1) as b:
                steps(segment(WIN), b, b)
                steps(segment(FOX), b + 1, b)
            steps(segment(WIN), DEC_BATCH - 1, DEC_BATCH - 1)
            steps(values_only(), None, DEC_BATCH - 1)
            sp.wait_ge(o_out, 2 * DEC_BATCH + 1)
            for kind in (FOX, WIN):
                sp.dma_start(a["o_s"][kind, :, :, SEQ:N_TOK].rearrange("q p n -> p q n"), o_t[:, kind]).then_inc(o_stored, 16)
            sp.wait_ge(o_stored, 32)

        @block.gpsimd
        def _(gp):
            per = DEC_BATCH // LF_GROUPS
            for i in range(LF_GROUPS):
                gp.dma_start(page_col[:, i:i + 1], a["page_table"][i * per:(i + 1) * per].rearrange("b n -> (b n)").unsqueeze(1)).then_inc(idx_in, 16)
            gp.memset(q_st[:].bitcast(F32), 0.0).then_inc(zeroed, 1)
            gp.wait_ge(idx_in, 16 * LF_GROUPS)
            for i in range(LF_GROUPS):
                gp.indirect_dma_start(lf_rows[:, i, :], None, a["cache_fox_logf"][0].rearrange("n k h -> n (k h)"),
                                      bass.IndirectOffsetOnAxis(ap=page_col[:, i:i + 1], axis=0)).then_inc(lf_gathered, 16)
                gp.wait_ge(lf_gathered, 16 * (i + 1))
            gp.sem_inc(g["v_lo"], PER_BATCH)

            def lay_queries(kind, b):
                gp.wait_ge(zeroed, 1)
                gp.wait_ge(parts_lo, 2)
                sets = slice(0, 1) if kind == FOX else slice(1, SETS)
                view = q_st[:, sets, :].rearrange("p s (q n) -> p s q n", n=144)
                for hh in range(2):
                    rows = slice(64 * hh, 64 * hh + 64)
                    for i, part in enumerate((qn_hi, qn_lo)):
                        at = i * HT + hh * DEC_SEQ
                        gp.tensor_copy(view[rows, :, :, at:at + DEC_SEQ],
                                       part[rows, sets, :, bass.ds(b * DEC_SEQ, DEC_SEQ)]).then_inc(q_ready[kind], 1)
                        gp.wait_ge(q_ready[kind], 4 * b + 2 * hh + i + 1)

            def stage(what, kind, j, b_keys, b_values):
                if what == "K" and kind == FOX:
                    done(gp, g["k_scored"], group_before(kind, b_keys, j))
                    src = sfx[:].rearrange("p b s x h -> p (b s) x h")[:, bass.ds(b_keys * N_PAGES + 2 * j, 2)]
                    gp.tensor_copy(sfx_wide[:, j % 2].rearrange("p i (x h t) -> p (i x h) t", x=2, h=HEADS),
                                   src.rearrange("p i x h -> p (i x h)").unsqueeze(2).to_broadcast([P, 4 * HEADS, DEC_SEQ])).then_inc(sfx_laid, 1)
                if what != "V":
                    return
                b = b_values
                index, slot, tiles = group_index(kind, b, j), j % 2, group_tiles(kind, j)
                src = raw_group("V", kind, j)
                done(gp, g["v_hi"], index)
                if j == N_GROUPS[kind] - 1:
                    rows = slice(0, new_rows[kind])
                    gp.tensor_tensor(vn_lo[rows, kind, :], vn_raw[rows, kind, :], vn_hi[rows, kind, :].bitcast(F32), ALU.subtract).then_inc(vn_split, 1)
                    gp.wait_ge(vn_split, 2 * b + kind + 1)
                gp.tensor_tensor(vv_lo[:, slot, 0:tiles, :], src, vv_hi[:, slot, 0:tiles, :].bitcast(F32), ALU.subtract).then_inc(g["v_lo"], 1)

            def steps(seg, b_keys, b_values):
                in_order(seg, {lambda *s: stage(*s, b_keys, b_values): 0})

            lay_queries(FOX, 0)
            lay_queries(WIN, 0)
            gp.wait_ge(parts_lo, 3)
            gp.tensor_copy(lfn_wide[:].rearrange("p (x t) -> p x t", t=DEC_SEQ),
                           lfn[:].rearrange("p x h -> p (x h)").unsqueeze(2).to_broadcast([N_SAMPLE, 2 * HEADS, DEC_SEQ])).then_inc(lfn_laid, 1)
            gp.wait_ge(lfn_laid, 1)
            gp.wait_ge(sfx_lo, 1)
            steps(keys_only(), 0, None)
            with gp.Fori(0, DEC_BATCH - 1) as b:
                done(gp, g["k_scored"], group_index(FOX, b, N_GROUPS[FOX] - 1))
                lay_queries(FOX, b + 1)
                steps(segment(WIN), b, b)
                done(gp, g["k_scored"], group_index(WIN, b, N_GROUPS[WIN] - 1))
                lay_queries(WIN, b + 1)
                steps(segment(FOX), b + 1, b)
            steps(segment(WIN), DEC_BATCH - 1, DEC_BATCH - 1)
            steps(values_only(), None, DEC_BATCH - 1)

        flat = ktp[:].rearrange("p a q n -> p (a q n)")
        WIDE = HEADS * LF_GROUPS * P

        def batches(eng, steps):
            steps(keys_only(), 0, None)
            with eng.Fori(0, DEC_BATCH - 1) as b:
                steps(segment(WIN), b, b)
                steps(segment(FOX), b + 1, b)
            steps(segment(WIN), DEC_BATCH - 1, DEC_BATCH - 1)
            steps(values_only(), None, DEC_BATCH - 1)

        @block.scalar
        def _(act):
            for s in (g["k_hi"], g["v_hi"], g["p_done"], g["p_hi"]):
                act.sem_inc(s, PER_BATCH)
            act.wait_ge(in_small, N_SMALL)
            for dst, src in ((qn_hi[:], qn_raw[:]), (kn_hi[:], kn_raw[:]), (lfn[:, 0, :], lfn_raw[:]),
                             (new_tri[:], new_tri_raw[:]), (shift[:], shift_raw[:])):
                act.activation(dst, src, ACT.Copy).then_inc(parts_hi, 1)
            act.wait_ge(sfx_summed, 1)
            act.activation(sfx[:, :, :, 0, :], flat.rearrange("p (h b s) -> p b s h", h=HEADS, b=DEC_BATCH), ACT.Copy).then_inc(sfx_hi, 1)

            def keys_hi(what, kind, j, bk, bv):
                if what != "K":
                    return
                slot, n = j % 2, group_tiles(kind, j) * P
                done(act, g["k_turned"], group_index(kind, bk, j))
                done(act, g["k_scored"], group_before(kind, bk, j))
                if group_new(kind, j) is not None:
                    act.activation(kt_hi[:, slot, :, n:n + DEC_SEQ],
                                   kn_hi[:, group_set(kind, j), :, bass.ds(bk * DEC_SEQ, DEC_SEQ)].bitcast(F32), ACT.Copy)
                act.activation(kt_hi[:, slot, :, 0:n], ktp[:, slot, :, 0:n], ACT.Copy).then_inc(g["k_hi"], 1)

            def values_hi(what, kind, j, bk, bv):
                if what != "V":
                    return
                slot, tiles, last = j % 2, group_tiles(kind, j), j == N_GROUPS[kind] - 1
                rows, cols, before = slice(0, new_rows[kind]), group_col(kind, j), group_before(kind, bv, j)
                if j == 0:
                    act.wait_ge(mx_neg[kind], bv + 1)
                done(act, g["p_turned"], before)
                if last:
                    act.activation(prob_new[:, kind, rows], scores[kind][:, main_cols[kind]:main_cols[kind] + new_rows[kind]], ACT.Exp,
                                   bias=neg_mx[:, kind:kind + 1], accum_out=den_parts[:, kind, j + 1:j + 2])
                act.activation(prob[:, slot, 0:tiles * P], scores[kind][:, cols:cols + tiles * P], ACT.Exp,
                               bias=neg_mx[:, kind:kind + 1], accum_out=den_parts[:, kind, j:j + 1]).then_inc(g["p_done"], 1)
                raw_arrived(act, "V", kind, bv, j)
                done(act, g["v_summed"], before)
                if last:
                    act.wait_ge(vn_in[kind], 16 * (1 if kind == FOX else len(DIL)) * (bv + 1))
                    act.activation(vn_hi[rows, kind, :], vn_raw[rows, kind, :], ACT.Copy)
                act.activation(vv_hi[:, slot, 0:tiles, :], raw_group("V", kind, j), ACT.Copy).then_inc(g["v_hi"], 1)

            def probs_hi(what, kind, j, bk, bv):
                if what != "V":
                    return
                slot, tiles, rows = j % 2, group_tiles(kind, j), slice(0, new_rows[kind])
                done(act, g["p_turned"], group_index(kind, bv, j))
                if j == N_GROUPS[kind] - 1:
                    act.activation(ptn[rows, kind, 0, :], pt_ps[rows, 2 * HT:3 * HT], ACT.Copy)
                act.activation(pt[:, slot, 0:tiles, 0, :], pt_ps[:, 0:tiles * HT].rearrange("p (i n) -> p i n", n=HT),
                               ACT.Copy).then_inc(g["p_hi"], 1)

            def scores_low(what, kind, j, bk, bv):
                if what == "K" and kind == FOX:
                    slot = j % 2
                    done(act, g["k_scored"], group_index(kind, bk, j))
                    done(act, g["s_done"], group_before(kind, bk, j))
                    wide = GROUP + (DEC_SEQ if group_new(kind, j) is not None else 0)
                    act.activation(s_tmp[:, slot, 0:wide], s_ps[HT:2 * HT, slot, 0:wide], ACT.Copy).then_inc(tmp_fox, 1)

            def out_low(what, kind, j, bk, bv):
                if what == "F":
                    act.wait_ge(r_den_done, 2 * bv + kind + 1)
                    done(act, g["v_summed"], group_index(kind, bv, N_GROUPS[kind] - 1))
                    act.activation(o_low[:], o_ps[HT:2 * HT, :], ACT.Copy).then_inc(o_low_done, 1)

            def steps(seg, bk, bv):
                in_order(seg, {lambda *s: probs_hi(*s, bk, bv): 1, lambda *s: keys_hi(*s, bk, bv): 0,
                               lambda *s: values_hi(*s, bk, bv): 0, lambda *s: out_low(*s, bk, bv): 0,
                               lambda *s: scores_low(*s, bk, bv): 2})

            batches(act, steps)

        @block.vector
        def _(ve):
            for s in (g["k_lo"], g["s_done"], g["p_lo"]):
                ve.sem_inc(s, PER_BATCH)
            ve.sem_inc(o_out, 1)
            for i, (dst, src, hi) in enumerate(((qn_lo[:], qn_raw[:], qn_hi[:]), (kn_lo[:], kn_raw[:], kn_hi[:]),
                                                (lfn[:, 1, :], lfn_raw[:], lfn[:, 0, :]))):
                ve.wait_ge(parts_hi, i + 1)
                ve.tensor_tensor(dst, src, hi.bitcast(F32), ALU.subtract).then_inc(parts_lo, 1)
            for i, dst in enumerate((lf_t, lf_later)):
                ve.wait_ge(lf_turned, i + 1)
                ve.tensor_copy(dst.rearrange("p h g n -> p (h g n)"), flat).then_inc(lf_copied, 1)
            ve.wait_ge(sfx_hi, 1)
            ve.tensor_tensor(sfx[:, :, :, 1, :], flat.rearrange("p (h b s) -> p b s h", h=HEADS, b=DEC_BATCH),
                             sfx[:, :, :, 0, :].bitcast(F32), ALU.subtract).then_inc(sfx_lo, 1)

            def keys_lo(what, kind, j, bk, bv):
                if what != "K":
                    return
                slot, n = j % 2, group_tiles(kind, j) * P
                done(ve, g["k_hi"], group_index(kind, bk, j))
                if group_new(kind, j) is not None:
                    ve.tensor_copy(kt_lo[:, slot, :, n:n + DEC_SEQ], kn_lo[:, group_set(kind, j), :, bass.ds(bk * DEC_SEQ, DEC_SEQ)])
                ve.tensor_tensor(kt_lo[:, slot, :, 0:n], ktp[:, slot, :, 0:n], kt_hi[:, slot, :, 0:n].bitcast(F32),
                                 ALU.subtract).then_inc(g["k_lo"], 1)

            def probs_lo(what, kind, j, bk, bv):
                if what != "V":
                    return
                slot, tiles, rows = j % 2, group_tiles(kind, j), slice(0, new_rows[kind])
                done(ve, g["p_hi"], group_index(kind, bv, j))
                if j == N_GROUPS[kind] - 1:
                    ve.tensor_tensor(ptn[rows, kind, 1, :], pt_ps[rows, 2 * HT:3 * HT], ptn[rows, kind, 0, :].bitcast(F32), ALU.subtract)
                ve.tensor_tensor(pt[:, slot, 0:tiles, 1, :], pt_ps[:, 0:tiles * HT].rearrange("p (i n) -> p i n", n=HT),
                                 pt[:, slot, 0:tiles, 0, :].bitcast(F32), ALU.subtract).then_inc(g["p_lo"], 1)

            def sum_scores(what, kind, j, bk, bv):
                if what != "K":
                    return
                slot, n, last = j % 2, group_tiles(kind, j) * P, N_GROUPS[kind] - 1
                cols, new = group_col(kind, j), group_new(kind, j)
                done(ve, g["k_scored"], group_index(kind, bk, j))
                done(ve, g["s_done"], group_before(kind, bk, j))
                if kind == FOX:
                    ve.wait_ge(tmp_fox, N_GROUPS[FOX] * bk + j + 1)
                if new is not None:
                    order = 4 * bk + group_set(kind, j)
                    done(ve, g["p_done"], group_index(kind, bk, last) - PER_BATCH)
                    m = mask_new[:] if kind == FOX else mask[:, WIN_COLS + new * DEC_SEQ:WIN_COLS + (new + 1) * DEC_SEQ]
                    low = s_tmp[:, slot, GROUP:] if kind == FOX else s_ps[HT:2 * HT, slot, n:n + DEC_SEQ]
                    ve.tensor_tensor(s_tmp[:, slot, GROUP:], low, m, ALU.add).then_inc(s_new_tmp, 1)
                    ve.wait_ge(s_new_tmp, order + 1)
                    at = main_cols[kind] + new * DEC_SEQ
                    hold(ve)
                    ve.tensor_tensor_reduce(out=scores[kind][:, at:at + DEC_SEQ], in0=s_ps[0:HT, slot, n:n + DEC_SEQ], in1=s_tmp[:, slot, GROUP:],
                                            scale=1.0, scalar=-3.0e38, op0=ALU.add, op1=ALU.max,
                                            accum_out=mx_parts[:, kind, last + 1 + new:last + 2 + new]).then_inc(s_new_done, 1)
                if kind == WIN:
                    ve.tensor_tensor(s_tmp[:, slot, 0:n], s_ps[HT:2 * HT, slot, 0:n], mask[:, cols:cols + n], ALU.add).then_inc(tmp_win, 1)
                    ve.wait_ge(tmp_win, N_GROUPS[WIN] * bk + j + 1)
                done(ve, g["p_done"], group_index(kind, bk, j) - PER_BATCH)
                hold(ve)
                ve.tensor_tensor_reduce(out=scores[kind][:, cols:cols + n], in0=s_ps[0:HT, slot, 0:n], in1=s_tmp[:, slot, 0:n],
                                        scale=1.0, scalar=-3.0e38, op0=ALU.add, op1=ALU.max,
                                        accum_out=mx_parts[:, kind, j:j + 1]).then_inc(g["s_done"], 1)
                if j == last:
                    done(ve, g["s_done"], group_index(kind, bk, j))
                    ve.tensor_reduce(mx[:, kind:kind + 1], mx_parts[:, kind, 0:last + (2 if kind == FOX else 1 + len(DIL))],
                                     AX.X, ALU.max).then_inc(mx_done[kind], 1)
                    ve.wait_ge(mx_done[kind], bk + 1)
                    ve.tensor_scalar(neg_mx[:, kind:kind + 1], mx[:, kind:kind + 1], -1.0, None, ALU.mult).then_inc(mx_neg[kind], 1)

            def out_rows(what, kind, j, bk, bv):
                if what != "F":
                    return
                job = 2 * bv + kind
                ve.tensor_reduce(den[:, kind:kind + 1], den_parts[:, kind, 0:N_GROUPS[kind] + 1], AX.X, ALU.add).then_inc(den_done, 1)
                ve.wait_ge(den_done, job + 1)
                ve.reciprocal(r_den[:, kind:kind + 1], den[:, kind:kind + 1]).then_inc(r_den_done, 1)
                ve.wait_ge(r_den_done, job + 1)
                ve.wait_ge(o_low_done, job + 1)
                ve.tensor_tensor(o_rows[:], o_ps[0:HT, :], o_low[:], ALU.add).then_inc(o_sum_done, 1)
                ve.wait_ge(o_sum_done, job + 1)
                ve.tensor_scalar(o_rows[:], o_rows[:], r_den[:, kind:kind + 1], None, ALU.mult).then_inc(o_done, 1)

            def out_diagonal(what, kind, j, bk, bv):
                if what != "F":
                    return
                ve.wait_ge(o_turned, 2 * bv + kind + 1)
                view = o_ps[:, 0:PAIRS * 80].rearrange("p (q n) -> p q n", n=80)
                for hh in range(2):
                    rows = slice(64 * hh, 64 * hh + 64)
                    last = ve.tensor_copy(o_t[rows, kind, :, bass.ds(bv * DEC_SEQ, DEC_SEQ)], view[rows, :, hh * DEC_SEQ:(hh + 1) * DEC_SEQ])
                last.then_inc(o_out, 1)

            def steps(seg, bk, bv):
                in_order(seg, {lambda *s: probs_lo(*s, bk, bv): 1, lambda *s: keys_lo(*s, bk, bv): 0,
                               lambda *s: out_rows(*s, bk, bv): 0, lambda *s: sum_scores(*s, bk, bv): 2,
                               lambda *s: out_diagonal(*s, bk, bv): 2})

            batches(ve, steps)

        @block.tensor
        def _(pe):
            for s in (g["k_turned"], g["k_scored"], g["p_turned"], g["v_summed"]):
                pe.sem_inc(s, PER_BATCH)
            pe.wait_ge(in_small, N_SMALL)
            pe.wait_ge(lf_gathered, 16 * LF_GROUPS)
            rows = [lf_rows[:, i, :].rearrange("p (k h) -> p h k", h=HEADS) for i in range(LF_GROUPS)]
            out = flat.rearrange("p (h g n) -> p h g n", h=HEADS, g=LF_GROUPS)
            for h in range(HEADS):
                for i in range(LF_GROUPS):
                    last = pe.transpose(out[:, h, i, :], rows[i][:, h, :], ident[:])
            last.then_inc(lf_turned, 1)
            pe.wait_ge(lf_copied, 1)
            for h in range(HEADS):
                for i in range(LF_GROUPS):
                    last = pe.matmul(out[:, h, i, :], rows[i][:, h, :], later[:], start=True, stop=True)
            last.then_inc(lf_turned, 1)
            pe.wait_ge(lf_copied, 2)
            for c in range(0, WIDE, 512):
                for i, (w, x) in enumerate(((tri, lf_t), (ones, lf_later))):
                    last = pe.matmul(flat[:, c:c + 512], w[:], x.rearrange("p h g n -> p (h g n)")[:, c:c + 512], start=(i == 0), stop=(i == 1))
            last.then_inc(sfx_summed, 1)
            pe.wait_ge(sfx_lo, 1)
            pe.wait_ge(parts_hi, SETUP_PARTS)
            pe.wait_ge(parts_lo, 3)

            def turn(what, kind, j, bk, bv):
                slot, tiles = j % 2, group_tiles(kind, j)
                if what == "K":
                    raw_arrived(pe, "K", kind, bk, j)
                    done(pe, g["k_lo"], group_before(kind, bk, j))
                    for i in range(tiles):
                        for q in range(PAIRS):
                            last = pe.transpose(ktp[:, slot, q, i * P:(i + 1) * P], raw_group("K", kind, j)[:, i, q * P:(q + 1) * P], ident[:])
                    last.then_inc(g["k_turned"], 1)
                if what == "V":
                    done(pe, g["p_done"], group_index(kind, bv, j))
                    done(pe, g["p_lo"], group_index(kind, bv, j) - 1)
                    hold(pe)
                    if j == N_GROUPS[kind] - 1:
                        r = new_rows[kind]
                        pe.transpose(pt_ps[0:r, 2 * HT:3 * HT], prob_new[:, kind, 0:r], ident[0:HT, 0:HT])
                    for i in range(tiles):
                        last = pe.transpose(pt_ps[:, i * HT:(i + 1) * HT], prob[:, slot, i * P:(i + 1) * P], ident[0:HT, 0:HT])
                    last.then_inc(g["p_turned"], 1)

            def sum_up(what, kind, j, bk, bv):
                slot, tiles = j % 2, group_tiles(kind, j)
                if what == "K":
                    n, new = tiles * P, group_new(kind, j)
                    wide = n + (DEC_SEQ if new is not None else 0)
                    if j == 0:
                        pe.wait_ge(q_ready[kind], 4 * bk + 4)
                    done(pe, g["k_lo"], group_index(kind, bk, j))
                    done(pe, g["s_done"], group_before(kind, bk, j))
                    if kind == FOX:
                        lots = []
                        pe.wait_ge(sfx_laid, N_GROUPS[FOX] * bk + j + 1)
                        for i in range(2):
                            lots.append((s_ps[:, slot, 0:GROUP], sfx_wide[:, slot, i, :], shift[:, (1 - i) * P:(3 - i) * P]))
                        if new is not None:
                            pe.wait_ge(lfn_laid, 1)
                            lots.append((s_ps[:, slot, n:wide], lfn_wide[:], new_tri[:, bass.ds(bk * DEC_SEQ, DEC_SEQ)]))
                    else:
                        lots = []
                    whole = [(s_ps[:, slot, 0:wide], q_st[:, group_set(kind, j), q * P:(q + 1) * P], x[:, slot, q, 0:wide])
                             for q in range(PAIRS) for x in (kt_hi, kt_lo)]
                    lots = whole[:1] + lots + whole[1:]
                    for i, (dst, w, x) in enumerate(lots):
                        last = pe.matmul(dst, w, x, start=(i == 0), stop=(i == len(lots) - 1))
                    last.then_inc(g["k_scored"], 1)
                if what == "V":
                    done(pe, g["p_lo"], group_index(kind, bv, j))
                    done(pe, g["v_lo"], group_index(kind, bv, j))
                    if j == 0:
                        pe.wait_ge(o_out, 2 * bv + kind + 1)
                    lots = []
                    if j == N_GROUPS[kind] - 1:
                        r = slice(0, new_rows[kind])
                        lots += [(ptn[r, kind, :, :].rearrange("p x n -> p (x n)"), x[r, kind, :]) for x in (vn_hi, vn_lo)]
                    lots += [(pt[:, slot, i, :, :].rearrange("p x n -> p (x n)"), x[:, slot, i, :]) for i in range(tiles) for x in (vv_hi, vv_lo)]
                    for i, (w, x) in enumerate(lots):
                        last = pe.matmul(o_ps[:], w, x, start=(j == 0 and i == 0), stop=(j == N_GROUPS[kind] - 1 and i == len(lots) - 1))
                    last.then_inc(g["v_summed"], 1)
                if what == "F":
                    pe.wait_ge(o_done, 2 * bv + kind + 1)
                    hold(pe)
                    for q in range(PAIRS):
                        last = pe.transpose(o_ps[:, q * HT:(q + 1) * HT], o_rows[:, q * P:(q + 1) * P], ident[0:HT, 0:HT])
                    last.then_inc(o_turned, 1)

            def steps(seg, bk, bv):
                in_order(seg, {lambda *s: turn(*s, bk, bv): 0, lambda *s: sum_up(*s, bk, bv): 2})

            batches(pe, steps)



def key_tiles(s, qt):
    return list(range(max(0, qt - 1), qt + 1)) if s == 1 else list(range(qt + 1))


def job_sets(kind):
    return (0,) if kind == FOX else tuple(range(1, SETS))


def prompt_units():
    return [(hh, qt, kind) for hh in range(2) for qt in range(Q_TILES) for kind in (FOX, WIN)]


def attend_prompt(nc, a, sem, ident):
    with ExitStack() as ctx:
        def sb(name, shape, dt=F32):
            return ctx.enter_context(nc.sbuf_tensor(name, shape, dt))

        def ps(name, shape):
            return ctx.enter_context(nc.psum_tensor(name, shape, F32))

        lf = sb("lf", [P, Q_TILES, HEADS])
        cum = sb("cum", [P, 2 * P])
        neg_c = sb("neg_c", [HEADS, SEQ])
        causal = sb("causal", [P, P])
        masks = sb("masks", [P, 2 * P + 2 * SEQ])
        q_raw = sb("q_raw", [P, SETS, SEQ])
        k_raw = sb("k_raw", [P, SETS, SEQ])
        v_raw = sb("v_raw3", [P, SETS, Q_TILES, P])
        bias = sb("bias", [P, 2, SEQ])
        bias_diag = sb("bias_diag", [P, 2, SEQ])
        q_hi = sb("q_hi", [P, 2, SETS, SEQ], F32R)
        q_lo = sb("q_lo", [P, 2, SETS, SEQ], F32R)
        k_hi = sb("k_hi3", [P, SETS, SEQ], F32R)
        k_lo = sb("k_lo3", [P, SETS, SEQ], F32R)
        v_hi = sb("v_hi3", [P, SETS, Q_TILES, P], F32R)
        v_lo = sb("v_lo3", [P, SETS, Q_TILES, P], F32R)
        s_fox = sb("s_fox3", [P, 2, SEQ])
        s_win = sb("s_win3", [P, 2, 2 * P + 2 * SEQ])
        mx_parts = sb("mx_parts3", [P, 2, 3])
        mx = sb("mx3", [P, 2])
        neg_mx = sb("neg_mx3", [P, 2])
        den = sb("den3", [P, 2, 2])
        r_den = sb("r_den3", [P, 2, 2])
        pt_hi = sb("pt_hi", [P, SETS, Q_TILES, SEQ], F32R)
        pt_lo = sb("pt_lo", [P, SETS, Q_TILES, SEQ], F32R)
        o_sb = sb("o_sb", [P, 2, SEQ])
        s_ps = ps("s_ps3", [P, SETS, 512])
        t_ps = ps("t_ps3", [P, 2, 512])
        o_ps = ps("o_ps3", [P, 2, 512])
        probs = (s_fox, s_win)

        names = ("in_small3", "c_summed", "c_copied", "c_stored", "q_zeroed3", "pair_in", "split_hi3", "split_lo3", "v_split3",
                 "bias_done", "s_summed3", "tmp3", "s_kept3", "mx_done3", "neg_done3", "exp_done3", "r_den3s", "norm_done3",
                 "t_turned3", "t_hi3", "t_lo3", "pv_done3", "o_copied3", "o_stored3", "o_free3", "held3")
        (in_small, c_summed, c_copied, c_stored, zeroed, pair_in, split_hi, split_lo, v_split, bias_done, s_summed, s_part,
         s_kept, mx_done, neg_done, exp_done, r_den_done, norm_done, t_turned, t_hi, t_lo, pv_done, o_copied, o_stored,
         o_free, held) = (sem(n) for n in names)
        N_SMALL, N_PAIR = 16 * 4, 16 * 13
        UNITS = len(prompt_units())
        CHUNKS = 2 * UNITS

        def segments(kind, qt):
            at, out = 0, []
            for s in job_sets(kind):
                out.append((s, key_tiles(s, qt), at))
                at += len(key_tiles(s, qt)) * P
            return out, at

        def unit_index(p, hh, qt, kind):
            return UNITS * p + 8 * hh + 2 * qt + kind

        def chunk_index(p, hh, qt, s):
            return CHUNKS * p + 16 * hh + 4 * qt + s

        def job_index(p, hh, kind):
            return 4 * p + 2 * hh + kind

        block = ctx.enter_context(nc.Block())

        @block.sync
        def _(sp):
            sp.dma_start(lf[:], a["lf_s"][0:SEQ].rearrange("(t p) h -> p t h", p=P)).then_inc(in_small, 16)
            sp.dma_start(cum[:], a["c_cum"]).then_inc(in_small, 16)
            sp.dma_start(causal[:], a["c_causal"]).then_inc(in_small, 16)
            sp.dma_start(masks[:], a["c_masks"]).then_inc(in_small, 16)
            sp.wait_ge(c_copied, 1)
            sp.dma_start(a["lc_s"], neg_c[:]).then_inc(c_stored, 16)
            sp.wait_ge(c_stored, 16)

            def load(p):
                for s in range(SETS):
                    sp.dma_start(q_raw[:, s, :], a["qt_s"][s, bass.ds(p, 1), :, 0:SEQ].rearrange("q p n -> p (q n)")).then_inc(pair_in, 16)
                    sp.dma_start(k_raw[:, s, :], a["kt_s"][s, bass.ds(p, 1), :, 0:SEQ].rearrange("q p n -> p (q n)")).then_inc(pair_in, 16)
                    sp.dma_start(v_raw[:, s], a["v_s"][s, 0:SEQ, bass.ds(p * P, P)].rearrange("(t p) n -> p t n", p=P)).then_inc(pair_in, 16)
                sp.dma_start(bias[:].rearrange("p h n -> p (h n)"),
                             a["lc_s"][bass.ds(2 * p, 2)].rearrange("h n -> (h n)").partition_broadcast(P)).then_inc(pair_in, 16)

            def store(p):
                sp.wait_ge(o_copied, 4 * p + 6)
                for kind in (FOX, WIN):
                    sp.dma_start(a["o_s"][kind, bass.ds(p, 1), :, 0:SEQ].rearrange("q p n -> p (q n)"), o_sb[:, kind, :]).then_inc(o_stored, 16)
                sp.wait_ge(o_stored, 32 * p + 32)
                sp.sem_inc(o_free, 1)

            sp.sem_inc(o_free, 1)
            load(0)
            with sp.Fori(0, PAIRS - 1) as p:
                sp.wait_ge(split_lo, 3 * p + 3)
                sp.sem_inc(held, 1)
                sp.wait_ge(v_split, p + 1)
                sp.wait_ge(pv_done, 4 * p + 6)
                sp.sem_inc(held, 1)
                load(p + 1)
                store(p)
            store(PAIRS - 1)

        @block.gpsimd
        def _(gp):
            gp.memset(q_hi[:].bitcast(F32), 0.0).then_inc(zeroed, 1)
            gp.memset(q_lo[:].bitcast(F32), 0.0).then_inc(zeroed, 1)
            gp.wait_ge(zeroed, 2)
            with gp.Fori(0, PAIRS) as p:
                gp.wait_ge(split_hi, 4 * p + 4)
                gp.tensor_tensor(v_lo[:], v_raw[:], v_hi[:].bitcast(F32), ALU.subtract).then_inc(v_split, 1)

                def normalise(hh, qt, kind):
                    _, width = segments(kind, qt)
                    x = probs[kind][:, qt % 2, 0:width]
                    gp.wait_ge(r_den_done, unit_index(p, hh, qt, kind) + 1)
                    gp.tensor_tensor(x, x, r_den[:, kind, qt % 2:qt % 2 + 1].to_broadcast([P, width]), ALU.mult).then_inc(norm_done, 1)

                in_order(prompt_units(), {normalise: 0})

        @block.scalar
        def _(act):
            act.sem_inc(o_copied, 2)
            act.wait_ge(c_summed, 1)
            act.activation(neg_c[:], o_ps[0:HEADS, 0, :], ACT.Copy).then_inc(c_copied, 1)
            act.wait_ge(zeroed, 2)
            with act.Fori(0, PAIRS) as p:
                act.wait_ge(pair_in, N_PAIR * p + N_PAIR)
                act.wait_ge(pv_done, 4 * p + 2)
                for hh in range(2):
                    rows = slice(64 * hh, 64 * hh + 64)
                    act.activation(q_hi[rows, hh], q_raw[rows], ACT.Copy).then_inc(split_hi, 1)
                act.activation(k_hi[:], k_raw[:], ACT.Copy).then_inc(split_hi, 1)
                act.activation(v_hi[:], v_raw[:], ACT.Copy).then_inc(split_hi, 1)

                def exponentials(hh, qt, kind):
                    index, (_, width) = unit_index(p, hh, qt, kind), segments(kind, qt)
                    x = probs[kind][:, qt % 2, 0:width]
                    act.wait_ge(neg_done, index + 1)
                    act.activation(x, x, ACT.Exp, bias=neg_mx[:, kind:kind + 1], accum_out=den[:, kind, qt % 2:qt % 2 + 1]).then_inc(exp_done, 1)

                def turned_hi(hh, qt, kind):
                    for s in job_sets(kind):
                        tiles, c = key_tiles(s, qt), chunk_index(p, hh, qt, s)
                        if qt == 0:
                            act.wait_ge(pv_done, job_index(p, hh, kind) + 1)
                        act.wait_ge(t_turned, c + 9)
                        act.activation(pt_hi[:, s, tiles[0]:tiles[-1] + 1, qt * P:(qt + 1) * P],
                                       t_ps[:, s % 2, 0:len(tiles) * P].rearrange("p (k n) -> p k n", n=P), ACT.Copy).then_inc(t_hi, 1)

                def outputs(hh, qt, kind):
                    if qt == Q_TILES - 1:
                        rows = slice(64 * hh, 64 * hh + 64)
                        if hh == 0:
                            act.wait_ge(o_free, p + 1)
                        act.wait_ge(pv_done, job_index(p, hh, kind) + 3)
                        act.activation(o_sb[rows, kind, :], o_ps[rows, kind, :], ACT.Copy).then_inc(o_copied, 1)

                in_order(prompt_units(), {exponentials: 0, turned_hi: 2, outputs: 4})

        @block.vector
        def _(ve):
            ve.sem_inc(s_kept, 2)
            ve.sem_inc(t_lo, 2)
            ve.wait_ge(in_small, N_SMALL)
            with ve.Fori(0, PAIRS) as p:
                for hh in range(2):
                    rows = slice(64 * hh, 64 * hh + 64)
                    ve.wait_ge(split_hi, 4 * p + hh + 1)
                    ve.tensor_tensor(q_lo[rows, hh], q_raw[rows], q_hi[rows, hh].bitcast(F32), ALU.subtract).then_inc(split_lo, 1)
                ve.wait_ge(split_hi, 4 * p + 3)
                ve.tensor_tensor(k_lo[:], k_raw[:], k_hi[:].bitcast(F32), ALU.subtract).then_inc(split_lo, 1)
                ve.tensor_tensor(bias_diag[:].rearrange("p h (t n) -> p (h t) n", n=P), bias[:].rearrange("p h (t n) -> p (h t) n", n=P),
                                 causal[:].unsqueeze(1).to_broadcast([P, 2 * Q_TILES, P]), ALU.add).then_inc(bias_done, 1)
                ve.wait_ge(bias_done, p + 1)

                def keep(hh, qt, kind):
                    index = unit_index(p, hh, qt, kind)
                    lots = []
                    for s, tiles, at in segments(kind, qt)[0]:
                        n = len(tiles) * P
                        if kind == FOX:
                            if qt:
                                lots.append((s_ps[:, 0, 0:qt * P], bias[:, hh, 0:qt * P], at, qt * P))
                            lots.append((s_ps[:, 0, qt * P:n], bias_diag[:, hh, qt * P:n], at + qt * P, P))
                        else:
                            end = (2 * P, 2 * P + SEQ, 2 * P + 2 * SEQ)[s - 1]
                            lots.append((s_ps[:, s, 0:n], masks[:, end - n:end], at, n))
                    ve.wait_ge(s_summed, index + 1)
                    ve.wait_ge(t_turned, chunk_index(p, hh, qt, 0) + (1 if kind == FOX else 4))
                    ve.sem_inc(held, 1)
                    for i, (x, y, at, n) in enumerate(lots):
                        last = ve.tensor_tensor_reduce(out=probs[kind][:, qt % 2, at:at + n], in0=x, in1=y, scale=1.0, scalar=-3.0e38,
                                                       op0=ALU.add, op1=ALU.max, accum_out=mx_parts[:, kind, i:i + 1])
                    last.then_inc(s_kept, 1)
                    ve.wait_ge(s_kept, index + 3)
                    ve.tensor_reduce(mx[:, kind:kind + 1], mx_parts[:, kind, 0:len(lots)], AX.X, ALU.max).then_inc(mx_done, 1)
                    ve.wait_ge(mx_done, index + 1)
                    ve.tensor_scalar(neg_mx[:, kind:kind + 1], mx[:, kind:kind + 1], -1.0, None, ALU.mult).then_inc(neg_done, 1)

                def denominators(hh, qt, kind):
                    ve.wait_ge(exp_done, unit_index(p, hh, qt, kind) + 1)
                    ve.reciprocal(r_den[:, kind, qt % 2:qt % 2 + 1], den[:, kind, qt % 2:qt % 2 + 1]).then_inc(r_den_done, 1)

                def turned_lo(hh, qt, kind):
                    for s in job_sets(kind):
                        tiles, c = key_tiles(s, qt), chunk_index(p, hh, qt, s)
                        at = (slice(None), s, slice(tiles[0], tiles[-1] + 1), slice(qt * P, (qt + 1) * P))
                        ve.wait_ge(t_hi, c + 1)
                        ve.tensor_tensor(pt_lo[at], t_ps[:, s % 2, 0:len(tiles) * P].rearrange("p (k n) -> p k n", n=P),
                                         pt_hi[at].bitcast(F32), ALU.subtract).then_inc(t_lo, 1)

                in_order(prompt_units(), {keep: 0, denominators: 1, turned_lo: 2})

        @block.tensor
        def _(pe):
            pe.sem_inc(pv_done, 2)
            pe.sem_inc(t_turned, 8)
            pe.wait_ge(in_small, N_SMALL)
            for m in range(Q_TILES):
                for j in range(m + 1):
                    x = cum[:, 0:P] if j == m else cum[:, P:2 * P]
                    last = pe.matmul(o_ps[0:HEADS, 0, m * P:(m + 1) * P], lf[:, j, :], x, start=(j == 0), stop=(j == m))
            last.then_inc(c_summed, 1)
            with pe.Fori(0, PAIRS) as p:
                pe.wait_ge(split_lo, 3 * p + 3)
                pe.wait_ge(v_split, p + 1)

                def score(hh, qt, kind):
                    index = unit_index(p, hh, qt, kind)
                    pe.wait_ge(s_kept, index + 1)
                    for s in job_sets(kind):
                        tiles = key_tiles(s, qt)
                        cols = slice(tiles[0] * P, (tiles[-1] + 1) * P)
                        for i, (q, k) in enumerate(((q_hi, k_hi), (q_lo, k_hi), (q_hi, k_lo))):
                            last = pe.matmul(s_ps[:, s, 0:len(tiles) * P], q[:, hh, s, qt * P:(qt + 1) * P], k[:, s, cols],
                                             start=(i == 0), stop=(i == 2))
                    last.then_inc(s_summed, 1)

                def turn(hh, qt, kind):
                    pe.wait_ge(norm_done, unit_index(p, hh, qt, kind) + 1)
                    for s, tiles, at in segments(kind, qt)[0]:
                        pe.wait_ge(t_lo, chunk_index(p, hh, qt, s) + 1)
                        for i in range(len(tiles)):
                            last = pe.transpose(t_ps[:, s % 2, i * P:(i + 1) * P], probs[kind][:, qt % 2, at + i * P:at + (i + 1) * P], ident[:])
                        last.then_inc(t_turned, 1)

                def weigh(hh, qt, kind):
                    if qt < Q_TILES - 1:
                        return
                    pe.wait_ge(t_lo, chunk_index(p, hh, qt, job_sets(kind)[-1]) + 3)
                    pe.wait_ge(o_copied, job_index(p, hh, kind) + 1)
                    lots = []
                    for s in job_sets(kind):
                        for kt in range(Q_TILES):
                            end = min(kt + 2, Q_TILES) if s == 1 else Q_TILES
                            for v, x in ((v_hi, pt_hi), (v_lo, pt_hi), (v_hi, pt_lo)):
                                lots.append((slice(kt * P, end * P), v[:, s, kt, :], x[:, s, kt, kt * P:end * P]))
                    whole = [x for x in lots if x[0] == slice(0, SEQ)]
                    lots = whole[:1] + [x for x in lots if x[0] != slice(0, SEQ)] + whole[1:]
                    for i, (cols, v, x) in enumerate(lots):
                        last = pe.matmul(o_ps[:, kind, cols], v, x, start=(i == 0), stop=(i == len(lots) - 1))
                    last.then_inc(pv_done, 1)

                in_order(prompt_units(), {score: 0, turn: 2, weigh: 3})


def finish(nc, a, sem, ident):
    with ExitStack() as ctx:
        def sb(name, shape, dt=F32):
            return ctx.enter_context(nc.sbuf_tensor(name, shape, dt))

        FF_GROUPS = D_FF // D_MODEL
        HALVES = 2
        left_hi, left_lo = (sb(n, [P, KT, TOK_PAD], F32R) for n in ("left_hi", "left_lo"))
        right_hi, right_lo = (sb(n, [P, KT, TOK_PAD], F32R) for n in ("right_hi", "right_lo"))
        o_raw = sb("o_raw", [P, KT, N_TOK])
        w_raw = sb("w_raw4", [P, 2, SLAB])
        w_hi = sb("w_hi4", [P, 2, SLAB], F32R)
        w_lo = sb("w_lo4", [P, 2, SLAB], F32R)
        gates = sb("gates4", [P, 2, 2, N_TOK])
        h = sb("h4", [P, TILES, D_MODEL])
        g2_row = sb("g2_row", [P, D_MODEL])
        sq = sb("sq4", [P, D_MODEL])
        ss, std, rstd = (sb(n, [P, TILES]) for n in ("ss4", "std4", "rstd4"))
        eps_col = sb("eps_col4", [P, 1])
        hn = sb("hn4", [P, 2, D_MODEL])
        first = sb("first4", [P, 2, N_TOK])
        second = sb("second4", [P, 2, N_TOK])
        acc = ctx.enter_context(nc.psum_tensor("acc4", [P, 8, 512], F32))

        (o_in, x_in, sample_in, g2_in, pad_zeroed, eps_set, o_hi_done, o_lo_done) = (
            sem(n) for n in ("o_in4", "x_in4", "sample_in4", "g2_in4", "pad_zeroed4", "eps_set4", "o_hi4", "o_lo4"))
        slab_loaded = [sem(f"slab_loaded4{i}") for i in range(2)]
        gate_in = [sem(f"gate_in4{i}") for i in range(2)]
        slab_hi_done, slab_lo_done, half_used, acc_done, branch_done = (
            sem(n) for n in ("slab_hi4", "slab_lo4", "half_used4", "acc_done4", "branch_done4"))
        both_gated, gated, mix_hi, mix_lo, h_added, h_squared, std_done, rstd_done, hn_done, hn_turned, hn_hi, hn_lo = (
            sem(n) for n in ("both_gated4", "gated4", "mix_hi4", "mix_lo4", "h_added4", "h_squared4", "std_done4", "rstd_done4",
                             "hn_done4", "hn_turned4", "hn_hi4", "hn_lo4"))
        held, up_done, relu_done, u_squared, u_hi, u_lo, y_stored = (
            sem(n) for n in ("held4", "up_done4", "relu_done4", "u_squared4", "u_hi4", "u_lo4", "y_stored4"))

        block = ctx.enter_context(nc.Block())

        def by_half(x):
            return x.rearrange("p (h n) -> p h n", h=HALVES)

        @block.sync
        def _(sp):
            def load_slab(n, slot, src):
                if slot is not None:
                    sp.wait_ge(slab_lo_done, n - 1)
                    sp.sem_inc(held, 1)
                else:
                    slot = n
                sp.dma_start(w_raw[:, slot, :].rearrange("p (k n) -> p k n", k=src.shape[1]), src).then_inc(slab_loaded[slot], 16)

            def branch_slab(n):
                w = (a["w_branch_a"], a["w_branch_b"])[n % 2][0]
                return w[:, (n // 2) * 512:(n // 2) * 512 + 512].rearrange("(k p) n -> p k n", p=P)

            load_slab(0, None, branch_slab(0))
            for kind in (FOX, WIN):
                sp.dma_start(o_raw[:, kind * PAIRS:(kind + 1) * PAIRS, :], a["o_s"][kind].rearrange("q p n -> p q n")).then_inc(o_in, 16)
                if kind == FOX:
                    load_slab(1, None, branch_slab(1))

            def load_gates(f):
                if f >= 2:
                    sp.wait_ge(gated, f - 1)
                sp.dma_start(gates[:, f % 2], a["gate_s"].rearrange("(b f) p n -> f p b n", b=2)[f]).then_inc(gate_in[f % 2], 16)

            load_gates(0)
            load_gates(1)
            sp.dma_start(h[:, 0:Q_TILES, :], a["x_prompt"][0].rearrange("(t p) d -> p t d", p=P)).then_inc(x_in, 16)
            sp.dma_start(h[0:N_SAMPLE, Q_TILES, :], a["x_sample"].rearrange("b t d -> (b t) d")).then_inc(sample_in, 16)
            sp.dma_start(g2_row[:], a["norm2_g"][0].partition_broadcast(P)).then_inc(g2_in, 16)
            for n in (2, 3):
                load_slab(n, n % 2, branch_slab(n))
            for f in range(2, KT):
                load_gates(f)
            for n in range(4):
                rows = a["w_out"][0][(n % 2) * 512:(n % 2) * 512 + 512, (n // 2) * 512:(n // 2) * 512 + 512]
                load_slab(n + 4, n % 2, rows.rearrange("(k p) n -> p k n", p=P))
            with sp.Fori(0, FF_GROUPS) as g:
                for i in range(4):
                    cols = a["w_up"][0][:, bass.ds(g * D_MODEL + i * 256, 256)]
                    load_slab(8 * g + 8 + i, i % 2, cols.rearrange("(k p) n -> p k n", p=P))
                for i in range(4):
                    rows = a["w_down"][0][bass.ds(g * D_MODEL + (i % 2) * 512, 512), (i // 2) * 512:(i // 2) * 512 + 512]
                    load_slab(8 * g + 12 + i, i % 2, rows.rearrange("(k p) n -> p k n", p=P))
            for c in range(2):
                cols = slice(c * 512, c * 512 + 512)
                y = a["y_prompt"][0].rearrange("(t p) d -> p t d", p=P)
                for t in range(TILES):
                    sp.wait_ge(h_added, 10 * FF_GROUPS + 5 * c + t + 1)
                    dst = y[:, t, cols] if t < Q_TILES else a["y_sample"].rearrange("b t d -> (b t) d")[:, cols]
                    sp.dma_start(dst, h[0:tile_rows(t), t, cols]).then_inc(y_stored, 16)
            sp.wait_ge(y_stored, 16 * 2 * TILES)

        @block.gpsimd
        def _(gp):
            gp.memset(h[N_SAMPLE:, Q_TILES, :], 0.0).then_inc(pad_zeroed, 1)
            gp.wait_ge(pad_zeroed, 1)
            gp.memset(right_hi[:, :, N_TOK:].bitcast(F32), 0.0).then_inc(pad_zeroed, 1)
            gp.memset(right_lo[:, :, N_TOK:].bitcast(F32), 0.0).then_inc(pad_zeroed, 1)
            with gp.Fori(0, 4 + 4 * FF_GROUPS) as pair:
                for slot in range(2):
                    gp.wait_ge(slab_hi_done, 2 * pair + slot + 1)
                    gp.tensor_tensor(w_lo[:, slot, :], w_raw[:, slot, :], w_hi[:, slot, :].bitcast(F32), ALU.subtract).then_inc(slab_lo_done, 1)

        @block.scalar
        def _(act):
            def slab_part(n, rounds, slot):
                act.wait_ge(slab_loaded[slot], 16 * rounds)
                act.activation(w_hi[:, slot, :], w_raw[:, slot, :], ACT.Copy).then_inc(slab_hi_done, 1)

            slab_part(0, 1, 0)
            for kind in (FOX, WIN):
                part = slice(kind * PAIRS, (kind + 1) * PAIRS)
                act.wait_ge(o_in, 32)
                act.activation(left_hi[:, part, 0:N_TOK], o_raw[:, part, :], ACT.Copy).then_inc(o_hi_done, 1)
                if kind == FOX:
                    slab_part(1, 1, 1)
            for f in range(KT):
                act.wait_ge(gated, f + 1)
                act.activation(right_hi[:, f, 0:N_TOK], first[:, f % 2, :], ACT.Copy).then_inc(mix_hi, 1)
                if f in (3, 7):
                    act.wait_ge(branch_done, f + 1)
                    slab_part(0, f // 4 + 2, 0)
                    slab_part(1, f // 4 + 2, 1)
            act.wait_ge(half_used, 1)
            slab_part(6, 4, 0)
            act.wait_ge(acc_done, 5)
            slab_part(7, 4, 1)

            def turned_hi(t):
                r = tile_rows(t)
                for u in (2 * t, 2 * t + 1):
                    act.wait_ge(hn_turned, u + 1)
                    act.activation(left_hi[:, 4 * (u % 2):4 * (u % 2) + 4, t * P:t * P + r],
                                   acc[:, 2 + u % 2, :].rearrange("p (k n) -> p k n", k=4)[:, :, 0:r], ACT.Copy).then_inc(hn_hi, 1)

            act.wait_ge(eps_set, 1)
            for t in range(TILES):
                act.wait_ge(h_added, 5 + t + 1)
                if t:
                    act.wait_ge(h_squared, t)
                act.activation(sq[:], h[:, t, :], ACT.Square, accum_out=ss[:, t:t + 1]).then_inc(h_squared, 1)
                act.wait_ge(h_squared, t + 1)
                act.activation(std[:, t:t + 1], ss[:, t:t + 1], ACT.Sqrt, scale=1.0 / D_MODEL, bias=eps_col[:]).then_inc(std_done, 1)
                if t:
                    turned_hi(t - 1)
            turned_hi(TILES - 1)
            with act.Fori(0, FF_GROUPS) as g:
                act.wait_ge(half_used, 2 * g + 2)
                slab_part(0, 4 * g + 5, 0)
                act.wait_ge(acc_done, 10 * g + 10)
                slab_part(1, 4 * g + 5, 1)
                for f in range(KT):
                    act.wait_ge(up_done, 8 * g + f + 1)
                    if f % 2:
                        slab_part(0, 4 * g + 6 + f // 4, (f // 2) % 2)
                    b = 2 + 2 * (f % 2)
                    act.activation(by_half(first[:, f % 2, :]), acc[:, b:b + 2, 0:HALF_TOK], ACT.Relu).then_inc(relu_done, 1)
                    act.wait_ge(u_squared, 8 * g + f + 1)
                    act.activation(right_hi[:, f, 0:N_TOK], second[:, f % 2, :], ACT.Copy).then_inc(u_hi, 1)
                act.wait_ge(half_used, 2 * g + 3)
                slab_part(6, 4 * g + 8, 0)
                act.wait_ge(acc_done, 10 * g + 15)
                slab_part(7, 4 * g + 8, 1)

        @block.vector
        def _(ve):
            ve.memset(eps_col[:], EPS).then_inc(eps_set, 1)
            for kind in (FOX, WIN):
                part = slice(kind * PAIRS, (kind + 1) * PAIRS)
                ve.wait_ge(o_hi_done, kind + 1)
                ve.tensor_tensor(left_lo[:, part, 0:N_TOK], o_raw[:, part, :], left_hi[:, part, 0:N_TOK].bitcast(F32), ALU.subtract).then_inc(o_lo_done, 1)
            for f in range(KT):
                ve.wait_ge(branch_done, f + 1)
                ve.wait_ge(gate_in[f % 2], 16 * (f // 2 + 1))
                if f >= 2:
                    ve.wait_ge(mix_lo, f - 1)
                for kind, out in ((FOX, first), (WIN, second)):
                    b = 4 * (f % 2) + 2 * kind
                    last = ve.tensor_tensor(by_half(out[:, f % 2, :]), acc[:, b:b + 2, 0:HALF_TOK], by_half(gates[:, f % 2, kind, :]), ALU.mult)
                last.then_inc(both_gated, 1)
                ve.wait_ge(both_gated, f + 1)
                ve.tensor_tensor(first[:, f % 2, :], first[:, f % 2, :], second[:, f % 2, :], ALU.add).then_inc(gated, 1)
                ve.wait_ge(mix_hi, f + 1)
                ve.tensor_tensor(right_lo[:, f, 0:N_TOK], first[:, f % 2, :], right_hi[:, f, 0:N_TOK].bitcast(F32), ALU.subtract).then_inc(mix_lo, 1)

            def add(t, c, count):
                cols = slice(c * 512, c * 512 + 512)
                ve.wait_ge(acc_done, count + 5 * c + t + 1)
                ve.tensor_tensor(h[:, t, cols], h[:, t, cols], acc[:, (5 * c + t) % 8, :], ALU.add).then_inc(h_added, 1)

            def turned_lo(t):
                r = tile_rows(t)
                for u in (2 * t, 2 * t + 1):
                    ve.wait_ge(hn_hi, u + 1)
                    part = (slice(None), slice(4 * (u % 2), 4 * (u % 2) + 4), slice(t * P, t * P + r))
                    ve.tensor_tensor(left_lo[part], acc[:, 2 + u % 2, :].rearrange("p (k n) -> p k n", k=4)[:, :, 0:r],
                                     left_hi[part].bitcast(F32), ALU.subtract).then_inc(hn_lo, 1)

            ve.wait_ge(x_in, 16)
            ve.wait_ge(sample_in, 16)
            ve.wait_ge(pad_zeroed, 3)
            for t in range(TILES):
                add(t, 0, 0)
            ve.wait_ge(g2_in, 16)
            for t in range(TILES):
                add(t, 1, 0)
                ve.wait_ge(std_done, t + 1)
                ve.reciprocal(rstd[:, t:t + 1], std[:, t:t + 1]).then_inc(rstd_done, 1)
                ve.wait_ge(rstd_done, t + 1)
                ve.wait_ge(h_added, 5 + t + 1)
                if t >= 2:
                    ve.wait_ge(hn_turned, 2 * t - 2)
                ve.scalar_tensor_tensor(out=hn[:, t % 2, :], in0=h[:, t, :], scalar=rstd[:, t:t + 1], in1=g2_row[:],
                                        op0=ALU.mult, op1=ALU.mult).then_inc(hn_done, 1)
                if t:
                    turned_lo(t - 1)
            turned_lo(TILES - 1)
            ve.sem_inc(u_lo, 2)
            with ve.Fori(0, FF_GROUPS) as g:
                for f in range(KT):
                    ve.wait_ge(relu_done, 8 * g + f + 3)
                    ve.wait_ge(u_lo, 8 * g + f + 1)
                    ve.tensor_tensor(second[:, f % 2, :], first[:, f % 2, :], first[:, f % 2, :], ALU.mult).then_inc(u_squared, 1)
                    ve.wait_ge(u_hi, 8 * g + f + 1)
                    ve.tensor_tensor(right_lo[:, f, 0:N_TOK], second[:, f % 2, :], right_hi[:, f, 0:N_TOK].bitcast(F32), ALU.subtract).then_inc(u_lo, 1)
                ve.wait_ge(h_added, 10 * g + 10)
                for c in range(2):
                    for t in range(TILES):
                        add(t, c, 10 * g + 10)

        @block.tensor
        def _(pe):
            pe.sem_inc(relu_done, 2)
            for f in range(KT):
                for kind in (FOX, WIN):
                    if f % 4 == 0:
                        pe.wait_ge(slab_lo_done, f // 2 + kind + 1)
                    if f == 0:
                        pe.wait_ge(o_lo_done, kind + 1)
                    if f >= 2:
                        pe.wait_ge(gated, f - 1)
                    w_parts = [w[:, kind, :].rearrange("p (k n) -> p k n", k=4)[:, :, (f % 4) * P:(f % 4) * P + P] for w in (w_hi, w_lo)]
                    for k in range(4):
                        for i, (w, x) in enumerate(((w_parts[0], left_hi), (w_parts[1], left_hi), (w_parts[0], left_lo))):
                            for half in range(HALVES):
                                last = pe.matmul(acc[:, 4 * (f % 2) + 2 * kind + half, 0:HALF_TOK], w[:, k, :],
                                                 x[:, kind * PAIRS + k, half * HALF_TOK:(half + 1) * HALF_TOK],
                                                 start=(k == 0 and i == 0), stop=(k == 3 and i == 2))
                last.then_inc(branch_done, 1)

            def natural(n, c, half, before):
                pe.wait_ge(slab_lo_done, n + 1)
                w_parts = [w[:, half, :].rearrange("p (k n) -> p k n", k=4) for w in (w_hi, w_lo)]
                for t in range(TILES):
                    if half == 0:
                        before(c, t)
                    for k in range(4):
                        kk = 4 * half + k
                        for i, (x, w) in enumerate(((right_hi, w_parts[0]), (right_hi, w_parts[1]), (right_lo, w_parts[0]))):
                            last = pe.matmul(acc[:, (5 * c + t) % 8, :], x[:, kk, t * P:t * P + P], w[:, k, :],
                                             start=(kk == 0 and i == 0), stop=(kk == KT - 1 and i == 2))
                    if half == 1:
                        last.then_inc(acc_done, 1)
                    elif t == TILES - 1:
                        last.then_inc(half_used, 1)

            def after_mix(c, t):
                if c == 0 and t in (0, 4):
                    pe.wait_ge(mix_lo, 7 + t // 4)
                if c == 1 and t >= 3:
                    pe.wait_ge(h_added, t - 2)

            pe.wait_ge(pad_zeroed, 3)
            for i in range(4):
                if i == 1:
                    pe.wait_ge(mix_lo, 8)
                natural(4 + i, i // 2, i % 2, after_mix)
            for u in range(2 * TILES):
                t = u // 2
                if u % 2 == 0:
                    pe.wait_ge(hn_done, t + 1)
                if u >= 2:
                    pe.wait_ge(hn_lo, u - 1)
                for k in range(4):
                    last = pe.transpose(acc[:, 2 + u % 2, k * P:k * P + P], hn[:, t % 2, (4 * (u % 2) + k) * P:(4 * (u % 2) + k + 1) * P], ident[:])
                last.then_inc(hn_turned, 1)
            pe.wait_ge(hn_lo, 2 * TILES)
            with pe.Fori(0, FF_GROUPS) as g:
                for f in range(KT):
                    slot = (f // 2) % 2
                    if f % 2 == 0:
                        pe.wait_ge(slab_lo_done, 8 * g + 8 + f // 2 + 1)
                    if f < 2:
                        pe.wait_ge(h_added, 10 * g + 5 + f)
                    pe.wait_ge(relu_done, 8 * g + f + 1)
                    w_parts = [w[:, slot, :].rearrange("p (k n) -> p k n", k=KT)[:, :, (f % 2) * P:(f % 2) * P + P] for w in (w_hi, w_lo)]
                    for k in range(KT):
                        for i, (w, x) in enumerate(((w_parts[0], left_hi), (w_parts[1], left_hi), (w_parts[0], left_lo))):
                            for half in range(HALVES):
                                last = pe.matmul(acc[:, 2 + 2 * (f % 2) + half, 0:HALF_TOK], w[:, k, :], x[:, k, half * HALF_TOK:(half + 1) * HALF_TOK],
                                                 start=(k == 0 and i == 0), stop=(k == KT - 1 and i == 2))
                    last.then_inc(up_done, 1)

                def after_up(c, t):
                    if c == 0 and t == 0:
                        pe.wait_ge(h_added, 10 * g + 10)
                        pe.wait_ge(u_lo, 8 * g + 6)
                    if c == 0 and t in (2, 4):
                        pe.wait_ge(relu_done, 8 * g + 9 + t // 4)
                    if c == 1 and t >= 3:
                        pe.wait_ge(h_added, 10 * g + 10 + t - 2)

                for i in range(4):
                    if i == 1:
                        pe.wait_ge(u_lo, 8 * g + 10)
                    natural(8 * g + 12 + i, i // 2, i % 2, after_up)


def rope_tables():
    half = HEAD_DIM // 2
    inv = (ROPE_THETA ** (-np.arange(half) / half)).astype(np.float32)
    pos = np.zeros((TILES, P), np.float32)
    pos[:Q_TILES] = np.arange(SEQ).reshape(Q_TILES, P)
    pos[Q_TILES, :N_SAMPLE] = PAST_LEN + np.arange(N_SAMPLE) % DEC_SEQ
    ang = (pos[:, :, None] * inv.astype(np.float32)).astype(np.float64)
    cos, sin = np.cos(ang).astype(np.float32), np.sin(ang).astype(np.float32)
    c = np.ones((SETS, TILES, P, HEAD_DIM), np.float32)
    s = np.zeros((SETS, TILES, P, HEAD_DIM), np.float32)
    c[1:] = np.concatenate([cos, cos], -1)
    s[1:] = np.concatenate([-sin, sin], -1)
    return c.transpose(2, 0, 1, 3).copy(), s.transpose(2, 0, 1, 3).copy()


def constants():
    cos, sin = rope_tables()
    k = np.arange(P)
    tri = (k[:, None] > k[None, :])
    slot, batch = k % N_PAGES, k // N_PAGES
    later = (slot[:, None] > slot[None, :]) & (batch[:, None] == batch[None, :])
    shift = np.zeros((P, 3 * P))
    shift[:, P:2 * P] = np.eye(P)
    t = np.arange(HT) % DEC_SEQ
    fill = lambda keep: np.where(keep, 0.0, NEG)
    new = np.arange(DEC_SEQ)
    win = []
    for g, r, n in WIN_GROUPS:
        d = DIL[g][1]
        for i in range(n):
            key = k * d + r + i
            win.append(fill((key[None, :] >= t[:, None]) & ((key[None, :] - t[:, None]) % d == 0)))
    for _, d in DIL:
        win.append(fill((new[None, :] <= t[:, None]) & ((t[:, None] - new[None, :]) % d == 0)))
    n = np.arange(N_SAMPLE)
    new_tri = np.where((n[:, None] // DEC_SEQ == n[None, :] // DEC_SEQ) & (n[:, None] <= n[None, :]), -1.0, 0.0)
    d = k[:, None] - k[None, :]
    causal = fill(d >= 0)
    masks = [fill(d <= 0), causal]
    for _, r in DIL[1:]:
        masks += [fill(d % r == 0)] * 3 + [fill((d >= 0) & (d % r == 0))]
    cum = np.concatenate([np.where(d <= 0, -1.0, 0.0), np.full((P, P), -1.0)], 1)
    out = dict(c_cum=cum, c_causal=causal, c_masks=np.concatenate(masks, 1), c_ident=np.eye(P), c_cos=cos, c_sin=sin, c_tri=tri, c_ones=np.ones((P, P)), c_later=later, c_shift=shift,
               c_mask_win=np.concatenate(win, 1), c_mask_new=fill(new[None, :] <= t[:, None]), c_new_tri=new_tri)
    return {name: np.ascontiguousarray(x, np.float32) for name, x in out.items()}


def output_shapes():
    kv = (HEADS, HEAD_DIM)
    out = dict(
        y_prompt=(1, SEQ, D_MODEL), y_sample=(DEC_BATCH, DEC_SEQ, D_MODEL),
        fox_k_prompt=(1, 1, SEQ, *kv), fox_v_prompt=(1, 1, SEQ, *kv), fox_logf_prompt=(1, 1, SEQ, HEADS))
    for g, (w, _) in enumerate(DIL):
        out[f"win{g + 1}_kv_prompt"] = (1, 1, min(w, SEQ), 2, *kv)
    out |= dict(fox_k_sample=(1, DEC_BATCH, DEC_SEQ, *kv), fox_v_sample=(1, DEC_BATCH, DEC_SEQ, *kv),
                fox_logf_sample=(1, DEC_BATCH, DEC_SEQ, HEADS))
    for g, (w, _) in enumerate(DIL):
        out[f"win{g + 1}_kv_sample"] = (1, DEC_BATCH, min(w, PAST_LEN), 2, *kv)
    return out


SCRATCH = dict(qt_s=(SETS, PAIRS, P, TOK_PAD), kt_s=(SETS, PAIRS, P, TOK_PAD), v_s=(SETS, N_TOK, D_HEADS),
               gate_s=(GATE_TILES, P, N_TOK), lf_s=(TOK_PAD, HEADS), o_s=(2, PAIRS, P, N_TOK), lc_s=(HEADS, SEQ))


def build(nc, aps, scratch_kind=None):
    scratch = {}
    for name, shape in SCRATCH.items():
        scratch[name] = (nc.dram_tensor(name, shape, F32, kind=scratch_kind) if scratch_kind else nc.dram_tensor(name, shape, F32)).ap()
    a = {**aps, **scratch}
    for name, form in (("windows", "cache_win{}_kv"), ("win_prompt", "win{}_kv_prompt"), ("win_sample", "win{}_kv_sample")):
        a[name] = [aps[form.format(n + 1)] for n in range(len(DIL))]
    with nc.sbuf_tensor("ident", [P, P], F32) as ident:
        for phase in (project_tokens, attend_sample, attend_prompt, finish):
            with nc.cleanup_on_exit():
                phase(nc, a, nc.alloc_semaphore, ident)


def kernel(**inputs):
    import concourse.bacc as bacc
    from concourse.bass_utils import run_bass_kernel_spmd

    nc = bacc.Bacc("TRN2", target_bir_lowering=False, num_devices=1)
    arrays, aps = {}, {}
    for name, x in (inputs | constants()).items():
        x = np.ascontiguousarray(x)
        arrays[f"in_{name}"] = x
        aps[name] = nc.dram_tensor(f"in_{name}", x.shape, mybir.dt.from_np(x.dtype), kind="ExternalInput").ap()
    for name, shape in output_shapes().items():
        aps[name] = nc.dram_tensor(f"out_{name}", shape, F32, kind="ExternalOutput").ap()
    build(nc, aps)
    got = run_bass_kernel_spmd(nc, [arrays], core_ids=[0]).results[0]
    return tuple(got[f"out_{name}"] for name in output_shapes())
```
